# Optimizing a Trainium2 kernel written in Bass

```python
import math
import jax, jax.numpy as jnp
from jax import lax
import numpy as np

D_MODEL = 1024
BATCH = 1
SEQ = 256
DEPTH = 2

N_MIXERS = 2
N_HEADS = 16
HEAD_DIM = 64
NSA_KV_GROUPS = 4
NSA_Q_PER_GROUP = N_HEADS // NSA_KV_GROUPS
CMP_BLOCK = 32
CMP_STRIDE = 16
CMP_HIDDEN = 256
SEL_BLOCK = 64
SEL_TOPK = 16
SEL_Q_CHUNK = 64
WINDOW = 512
Q_BLOCK = 128
NUM_BUCKETS = 32
MAX_DISTANCE = 128
D_FF = 2816
RMS_EPS = 1e-6
NEG_INF = -1e30
FORCED_SCORE = 1e9
Q_DIM = N_HEADS * HEAD_DIM
KV_DIM = NSA_KV_GROUPS * HEAD_DIM
NSA_IN_DIM = Q_DIM + 6 * KV_DIM + 3 * N_HEADS
FOX_IN_DIM = 3 * Q_DIM + N_HEADS
N_NSA_LAYERS = (DEPTH + 1) // 2
N_FOX_LAYERS = DEPTH // 2

kernel_name = "nsa_fox_macaron_sandwich_hybrid"

def rms_norm(x, g):
    xf = x.astype(jnp.float32)
    y = xf * lax.rsqrt(jnp.mean(xf * xf, axis=-1, keepdims=True) + RMS_EPS)
    return (y * g.astype(jnp.float32)).astype(x.dtype)

def swiglu(x, w_gate, w_up, w_down):
    return (jax.nn.silu(x @ w_gate) * (x @ w_up)) @ w_down

def t5_bucket(rel):
    n = jnp.maximum(rel, 0)
    max_exact = NUM_BUCKETS // 2
    nf = jnp.maximum(n, 1).astype(jnp.float32)
    large = max_exact + (jnp.log(nf / max_exact) / math.log(MAX_DISTANCE / max_exact)
                         * (NUM_BUCKETS - max_exact)).astype(jnp.int32)
    large = jnp.minimum(large, NUM_BUCKETS - 1)
    return jnp.where(n < max_exact, n, large)

def masked_softmax(logits, mask):
    logits = jnp.where(mask, logits.astype(jnp.float32), NEG_INF)
    p = jax.nn.softmax(logits, axis=-1)
    return jnp.where(mask, p, 0.0)

def nsa_mixer(h, w_in, cmp_pe, cmp_w1, cmp_b1, cmp_w2, w_out, rel_bias):
    B, S, _ = h.shape
    G, R, dh = NSA_KV_GROUPS, NSA_Q_PER_GROUP, HEAD_DIM
    scale = dh ** -0.5
    splits = np.cumsum([Q_DIM] + [KV_DIM] * 6).tolist()
    q, kc, vc, ks, vs, kw, vw, gates = jnp.split(h @ w_in, splits, axis=-1)
    q = q.reshape(B, S, G, R, dh).transpose(0, 2, 3, 1, 4)
    to_kv = lambda a: a.reshape(B, S, G, dh).transpose(0, 2, 1, 3)
    kc, vc, ks, vs, kw, vw = map(to_kv, (kc, vc, ks, vs, kw, vw))
    t_np = np.arange(S)

    nc = (S - CMP_BLOCK) // CMP_STRIDE + 1
    blk_idx = np.arange(nc)[:, None] * CMP_STRIDE + np.arange(CMP_BLOCK)[None, :]

    def compress(a, pe, w1, b1, w2):
        blocks = a[:, :, blk_idx] + pe
        flat = blocks.reshape(B, G, nc, CMP_BLOCK * dh)
        return jax.nn.gelu(flat @ w1 + b1) @ w2

    k_cmp = compress(kc, cmp_pe[0], cmp_w1[0], cmp_b1[0], cmp_w2[0])
    v_cmp = compress(vc, cmp_pe[1], cmp_w1[1], cmp_b1[1], cmp_w2[1])
    blk_end = np.arange(nc) * CMP_STRIDE + CMP_BLOCK - 1
    rel_c = t_np[:, None] - blk_end[None, :]
    mask_c = rel_c >= 0
    bias_c = jnp.transpose(rel_bias[t5_bucket(jnp.asarray(rel_c))], (2, 0, 1)).reshape(G, R, S, nc)
    logits_c = jnp.einsum('bgrsd,bgcd->bgrsc', q, k_cmp) * scale + bias_c
    p_c = masked_softmax(logits_c, mask_c)
    o_cmp = jnp.einsum('bgrsc,bgcd->bgrsd', p_c.astype(v_cmp.dtype), v_cmp)

    n_sel = S // SEL_BLOCK
    c_start = np.arange(nc)[:, None] * CMP_STRIDE
    j_np = np.arange(n_sel)[None, :]
    overlap = ((c_start < (j_np + 1) * SEL_BLOCK) & (c_start + CMP_BLOCK > j_np * SEL_BLOCK)).astype(np.float32)
    imp = jnp.einsum('bgrsc,cj->bgsj', p_c, jnp.asarray(overlap))
    cur = (t_np // SEL_BLOCK)[:, None]
    forced = (j_np == 0) | (j_np == cur) | (j_np == cur - 1)
    valid_blk = j_np <= cur
    imp = jnp.where(forced, FORCED_SCORE, jnp.where(valid_blk, imp, NEG_INF))
    k_eff = min(SEL_TOPK, n_sel)
    _, sel_idx = lax.top_k(imp, k_eff)

    k_blocks = ks.reshape(B, G, n_sel, SEL_BLOCK, dh)
    v_blocks = vs.reshape(B, G, n_sel, SEL_BLOCK, dh)
    tbl = jnp.transpose(rel_bias.reshape(NUM_BUCKETS, G, R), (1, 0, 2))
    b_ix = jnp.arange(B)[:, None, None, None]
    g_ix = jnp.arange(G)[None, :, None, None]
    C = SEL_Q_CHUNK
    n_ch = S // C

    def sel_chunk(args):
        q_c, idx_c, t_c = args
        kg = k_blocks[b_ix, g_ix, idx_c]
        vg = v_blocks[b_ix, g_ix, idx_c]
        pos = idx_c[..., None] * SEL_BLOCK + jnp.arange(SEL_BLOCK)
        rel = t_c[None, None, :, None, None] - pos
        bias = jnp.moveaxis(tbl[g_ix[..., None], t5_bucket(rel)], -1, 2)
        logits = jnp.einsum('bgrcd,bgckld->bgrckl', q_c, kg) * scale + bias
        mask = (rel >= 0)[:, :, None].reshape(B, G, 1, C, -1)
        p = masked_softmax(logits.reshape(B, G, R, C, -1), mask).reshape(logits.shape)
        return jnp.einsum('bgrckl,bgckld->bgrcd', p.astype(vg.dtype), vg)

    q_x = jnp.moveaxis(q.reshape(B, G, R, n_ch, C, dh), 3, 0)
    idx_x = jnp.moveaxis(sel_idx.reshape(B, G, n_ch, C, k_eff), 2, 0)
    t_x = jnp.arange(S).reshape(n_ch, C)
    o_sel = lax.map(sel_chunk, (q_x, idx_x, t_x))
    o_sel = jnp.moveaxis(o_sel, 0, 3).reshape(B, G, R, S, dh)

    n_qb = S // Q_BLOCK
    band = WINDOW + Q_BLOCK
    kw_p = jnp.pad(kw, ((0, 0), (0, 0), (WINDOW, 0), (0, 0)))
    vw_p = jnp.pad(vw, ((0, 0), (0, 0), (WINDOW, 0), (0, 0)))
    rel_w = np.arange(Q_BLOCK)[:, None] + WINDOW - np.arange(band)[None, :]
    band_mask = (rel_w >= 0) & (rel_w < WINDOW)
    bias_w = jnp.transpose(rel_bias[t5_bucket(jnp.asarray(rel_w))], (2, 0, 1)).reshape(G, R, Q_BLOCK, band)

    def win_block(args):
        q_b, start = args
        k_b = lax.dynamic_slice_in_dim(kw_p, start, band, axis=2)
        v_b = lax.dynamic_slice_in_dim(vw_p, start, band, axis=2)
        key_pos = start - WINDOW + jnp.arange(band)
        mask = band_mask & (key_pos >= 0)[None, :]
        logits = jnp.einsum('bgrqd,bgkd->bgrqk', q_b, k_b) * scale + bias_w
        p = masked_softmax(logits, mask)
        return jnp.einsum('bgrqk,bgkd->bgrqd', p.astype(v_b.dtype), v_b)

    qw_x = jnp.moveaxis(q.reshape(B, G, R, n_qb, Q_BLOCK, dh), 3, 0)
    o_win = lax.map(win_block, (qw_x, jnp.arange(n_qb) * Q_BLOCK))
    o_win = jnp.moveaxis(o_win, 0, 3).reshape(B, G, R, S, dh)

    g = jax.nn.sigmoid(gates.reshape(B, S, 3, G, R)).transpose(2, 0, 3, 4, 1)[..., None]
    o = g[0] * o_cmp + g[1] * o_sel + g[2] * o_win
    o = o.transpose(0, 3, 1, 2, 4).reshape(B, S, Q_DIM)
    return o @ w_out

def fox_mixer(h, w_in, b_f, w_out):
    B, S, _ = h.shape
    H, dh = N_HEADS, HEAD_DIM
    scale = dh ** -0.5
    q, k, v, f_logit = jnp.split(h @ w_in, [Q_DIM, 2 * Q_DIM, 3 * Q_DIM], axis=-1)
    heads = lambda a: a.reshape(B, S, H, dh).transpose(0, 2, 1, 3)
    q, k, v = heads(q), heads(k), heads(v)
    log_f = jax.nn.log_sigmoid((f_logit + b_f).astype(jnp.float32))
    cum = jnp.cumsum(log_f, axis=1).transpose(0, 2, 1)
    n_qb = S // Q_BLOCK
    key_pos = jnp.arange(S)

    def blk(args):
        q_b, cum_b, start = args
        decay = cum_b[..., None] - cum[:, :, None, :]
        logits = jnp.einsum('bhqd,bhkd->bhqk', q_b, k).astype(jnp.float32) * scale + decay
        qpos = start + jnp.arange(Q_BLOCK)
        mask = key_pos[None, :] <= qpos[:, None]
        p = masked_softmax(logits, mask)
        return jnp.einsum('bhqk,bhkd->bhqd', p.astype(v.dtype), v)

    q_x = jnp.moveaxis(q.reshape(B, H, n_qb, Q_BLOCK, dh), 2, 0)
    c_x = jnp.moveaxis(cum.reshape(B, H, n_qb, Q_BLOCK), 2, 0)
    o = lax.map(blk, (q_x, c_x, jnp.arange(n_qb) * Q_BLOCK))
    o = o.transpose(1, 0, 3, 2, 4).reshape(B, S, Q_DIM)
    return o @ w_out

def setup_inputs(seed: int = 0) -> dict:
    key = jax.random.key(seed)
    ks = jax.random.split(key, 16)
    nrm = lambda k, shape, fan_in: jax.random.normal(k, shape, jnp.float32) * (fan_in ** -0.5)
    dh = HEAD_DIM
    return {
        "x": jax.random.normal(ks[0], (BATCH, SEQ, D_MODEL), jnp.float32),
        "norm_g": 1.0 + 0.05 * jax.random.normal(ks[1], (DEPTH, 6, D_MODEL), jnp.float32),
        "ffn_w_gate": nrm(ks[2], (DEPTH, 2, D_MODEL, D_FF), D_MODEL),
        "ffn_w_up": nrm(ks[3], (DEPTH, 2, D_MODEL, D_FF), D_MODEL),
        "ffn_w_down": nrm(ks[4], (DEPTH, 2, D_FF, D_MODEL), D_FF),
        "rel_bias": 0.5 * jax.random.normal(ks[5], (NUM_BUCKETS, N_HEADS), jnp.float32),
        "nsa_w_in": nrm(ks[6], (N_NSA_LAYERS, D_MODEL, NSA_IN_DIM), D_MODEL),
        "nsa_cmp_pe": 0.1 * jax.random.normal(ks[7], (N_NSA_LAYERS, 2, CMP_BLOCK, dh), jnp.float32),
        "nsa_cmp_w1": nrm(ks[8], (N_NSA_LAYERS, 2, CMP_BLOCK * dh, CMP_HIDDEN), CMP_BLOCK * dh),
        "nsa_cmp_b1": 0.01 * jax.random.normal(ks[9], (N_NSA_LAYERS, 2, CMP_HIDDEN), jnp.float32),
        "nsa_cmp_w2": nrm(ks[10], (N_NSA_LAYERS, 2, CMP_HIDDEN, dh), CMP_HIDDEN),
        "nsa_w_out": nrm(ks[11], (N_NSA_LAYERS, Q_DIM, D_MODEL), Q_DIM),
        "fox_w_in": nrm(ks[12], (N_FOX_LAYERS, D_MODEL, FOX_IN_DIM), D_MODEL),
        "fox_b_f": 2.0 + 0.1 * jax.random.normal(ks[13], (N_FOX_LAYERS, N_HEADS), jnp.float32),
        "fox_w_out": nrm(ks[14], (N_FOX_LAYERS, Q_DIM, D_MODEL), Q_DIM),
    }

def reference(x, norm_g, ffn_w_gate, ffn_w_up, ffn_w_down, rel_bias, nsa_w_in, nsa_cmp_pe,
              nsa_cmp_w1, nsa_cmp_b1, nsa_cmp_w2, nsa_w_out, fox_w_in, fox_b_f, fox_w_out):
    h = x
    for i in range(DEPTH):
        g = norm_g[i]
        j = i // N_MIXERS
        y = swiglu(rms_norm(h, g[0]), ffn_w_gate[i, 0], ffn_w_up[i, 0], ffn_w_down[i, 0])
        h = h + 0.5 * rms_norm(y, g[1])
        u = rms_norm(h, g[2])
        if i % N_MIXERS == 0:
            y = nsa_mixer(u, nsa_w_in[j], nsa_cmp_pe[j], nsa_cmp_w1[j], nsa_cmp_b1[j],
                          nsa_cmp_w2[j], nsa_w_out[j], rel_bias)
        else:
            y = fox_mixer(u, fox_w_in[j], fox_b_f[j], fox_w_out[j])
        h = h + rms_norm(y, g[3])
        y = swiglu(rms_norm(h, g[4]), ffn_w_gate[i, 1], ffn_w_up[i, 1], ffn_w_down[i, 1])
        h = h + 0.5 * rms_norm(y, g[5])
    return h


_drawn_inputs = setup_inputs


def setup_inputs(seed=0):
    import zlib

    import numpy as np

    out = dict(_drawn_inputs(seed))
    spreads = {}
    factors = {'nsa_cmp_b1': 6.62, 'fox_b_f': 30.544}
    for name, (base, spread) in spreads.items():
        noise = np.random.default_rng([zlib.crc32(name.encode()), seed]).standard_normal(out[name].shape)
        drawn = base * np.exp(spread * noise) if base else spread * noise
        out[name] = __import__('jax').numpy.asarray(drawn.astype(out[name].dtype))
    for name, factor in factors.items():
        out[name] = (out[name] * factor).astype(out[name].dtype)
    return out
```

```python
from contextlib import ExitStack

import numpy as np

import concourse.bass as bass
from concourse import mybir

F32 = mybir.dt.float32
F32R = mybir.dt.float32r
ALU = mybir.AluOpType
ACT = mybir.ActivationFunctionType
AX = mybir.AxisListType

P = 128
D = 1024
S = 256
KT = D // P
TT = S // P
FF = 2816
UC = 256
NCH = FF // UC
H = 16
DH = 64
G = 4
CB, CS = 32, 16
NC = (S - CB) // CS + 1
CP = 32
HID = 256
NB = 32
NEG = -1e30
EPS = 1e-6
RING = 3
SCORES = S + P

KINDS = ["ffn", "nsa", "ffn", "ffn", "fox", "ffn"]
UNITS = {"ffn": 3 * NCH, "nsa": 14, "fox": 16}
U0 = [sum(UNITS[k] for k in KINDS[:s]) for s in range(len(KINDS))]
NUNITS = sum(UNITS[k] for k in KINDS)
NSUB = len(KINDS)
FFN_OF = {0: 0, 2: 1, 3: 2, 5: 3}
WHICH = [(0, 0), None, (0, 1), (1, 0), None, (1, 1)]
NORM = [(0, 0), (0, 2), (0, 4), (1, 0), (1, 2), (1, 4)]

C_ID, C_J, C_MASK, C_VALID, C_A1, C_A2, C_R, C_NEG = 0, 128, 256, 512, 514, 530, 546, 548
C_END = 564


def t5_bucket(rel):
    n = np.maximum(rel, 0)
    nf = np.maximum(n, 1).astype(np.float32)
    large = 16 + (np.log(nf / np.float32(16)) / np.float32(np.log(8.0)) * np.float32(16)).astype(np.int32)
    return np.where(n < 16, n, np.minimum(large, NB - 1))


def tables():
    c = np.zeros((P, C_END), np.float32)
    c[:, C_ID:C_ID + P] = np.eye(P)
    c[:, C_J:C_J + P] = np.eye(P)[::-1]
    p, j = np.arange(P)[:, None], np.arange(S)[None, :]
    c[:, C_MASK:C_MASK + S] = np.where(P + p - j >= 0, 0.0, NEG)
    for t in range(TT):
        c[:, C_VALID + t] = np.arange(P) + t * P >= CB - 1
    for h in range(H):
        c[h, C_A1 + h] = 1.0
        c[H + h, C_A2 + h] = 1.0
    c[H:2 * H, C_R] = -1.0
    c[0:H, C_R + 1] = 1.0
    c[NB, C_NEG:C_NEG + H] = NEG

    def onehot(rel):
        o = np.zeros((NB + 1, len(rel)), np.float32)
        o[np.where(rel < 0, NB, t5_bucket(rel)), np.arange(len(rel))] = 1.0
        return o

    near = onehot(np.arange(2 * S) - S)
    back = onehot(S - 1 - np.arange(S + P))
    return c, np.concatenate([near, back], 1)


def trunk(nc, x, norm_g, w_gate, w_up, w_down, rel_bias, nsa_in, cmp_pe, cmp_w1, cmp_b1, cmp_w2,
          nsa_out, fox_in, fox_bf, fox_out, consts, onehots, out, scratch):
    with ExitStack() as ctx:
        def sb(name, shape, dt=F32):
            return ctx.enter_context(nc.sbuf_tensor(name, shape, dt))

        def sem(name):
            return ctx.enter_context(nc.semaphore(name))

        raw = sb("raw", [P, RING, 2048])
        whi = sb("whi", [P, RING, 2048], F32R)
        wlo = sb("wlo", [P, RING, 2048], F32R)
        res = sb("res", [P, TT, D])
        xhi = sb("xhi", [P, KT, S], F32R)
        xlo = sb("xlo", [P, KT, S], F32R)
        hhi = sb("hhi", [P, 2, S], F32R)
        hlo = sb("hlo", [P, 2, S], F32R)
        work = sb("work", [P, 4 * SCORES])
        silu_sb = work[:, 0:512]
        prod_sb = work[:, 512:1024]
        prob = work[:, :].rearrange("p (b a n) -> p b a n", b=2, a=2)
        g_pre = sb("g_pre", [P, D])
        g_post = sb("g_post", [P, D])
        normed = sb("normed", [P, TT, D])
        big = sb("big", [P, 4096])
        skew = big[:, :].rearrange("p (h n) -> p h n", h=H)
        w1 = big[:, :].rearrange("p (k n) -> p k n", k=16)
        kF = big[:, 0:2048].rearrange("p (k n) -> p k n", k=KT)
        vF = big[:, 2048:4096].rearrange("p (t n) -> p t n", t=TT)
        bias = sb("bias", [P, H, S])
        kcv = work[:, 0:1024].rearrange("p (r g t) -> p r g t", r=2, g=2)
        kN = sb("kN", [P, 2, 2, S])
        kX = sb("kX", [P, 2, 2, S])
        vN = sb("vN", [P, 2, TT, S])
        qT = sb("qT", [P, KT, S])
        pairs = sb("pairs", [P, 1024])
        pairsv = pairs[:, :].rearrange("p (g t) -> p g t", g=G)
        probc = pairs[:, :].rearrange("p (t h c) -> p t h c", t=TT, h=H)
        near = pairs[0:NB + 1, 0:512]
        back = pairs[0:NB + 1, 512:896]
        flat = sb("flat", [P, 1024])
        flatv = flat[:, 0:16 * G * NC].rearrange("p (k n) -> p k n", k=16)
        gw = flat[:, 0:512].rearrange("p (k n) -> p k n", k=KT)
        probcT = flat[:, :].rearrange("p (g t) -> p g t", g=G)
        ghi = sb("ghi", [P, KT, DH], F32R)
        glo = sb("glo", [P, KT, DH], F32R)
        probT_buf = sb("probT_buf", [P, 4 * SCORES])
        probT = probT_buf[:, :].rearrange("p (b a n) -> p b a n", b=2, a=2)
        hidR = probT_buf[:, 0:1024].rearrange("p (m g r c) -> p m g r c", m=2, g=G, r=4)
        biasc = sb("biasc", [P, TT, H, NC])
        sc = sb("sc", [P, TT, H, NC])
        hid = sb("hid", [P, 2, G * NC])
        kcmp = sb("kcmp", [P, G * NC])
        vcmp = sb("vcmp", [P, G, DH])
        w2k = sb("w2k", [P, 2, 2, DH])
        w2v = sb("w2v", [P, 2, DH])
        cst = sb("cst", [P, C_END])
        tab = sb("tab", [NB + 1, H])
        small = sb("small", [36, P])
        smallT = sb("smallT", [P, 36])
        vrev = sb("vrev", [H, SCORES])
        gate_e = sb("gate_e", [P, TT, 48])
        gate = sb("gate", [P, TT, 48])
        fz = sb("fz", [P, TT, 32])
        fT = pairs[0:32, :].rearrange("p (k t) -> p k t", k=4)
        cum = flat[0:32, 0:S]
        rhsd = flat[0:32, S:2 * S]
        bf = sb("bf", [32, 1])
        ss = sb("ss", [P, 4 * NSUB])
        ms = sb("ms", [P, 4 * NSUB])
        rstd = sb("rstd", [P, 4 * NSUB])
        half = sb("half", [P, 1])
        nmax = sb("nmax", [P, 2, 2, TT])
        ssum = sb("ssum", [P, 2, 2, TT])
        rsum = sb("rsum", [P, 2, 2, TT])
        fac = sb("fac", [P, 2, 2, TT])
        cmx = sb("cmx", [P, TT, H])
        csum = sb("csum", [P, TT, H])
        cfac = sb("cfac", [P, TT, H])
        ps = ctx.enter_context(nc.psum_tensor("ps", [P, 8, 512], F32))
        ident = cst[:, C_ID:C_ID + P]
        YB, GB, UB, OB, MB = 0, 4, 5, 6, 7

        raw_in = [sem(f"raw_in{i}") for i in range(RING)]
        w_hi, w_lo, unit_done = sem("w_hi"), sem("w_lo"), sem("unit_done")
        res_in, cst_in, gw_in, small_in = sem("res_in"), sem("cst_in"), sem("gw_in"), sem("small_in")
        tab_in, oh_in, w2_in, bf_in = sem("tab_in"), sem("oh_in"), sem("w2_in"), sem("bf_in")
        gpre_in, gpost_in = sem("gpre_in"), sem("gpost_in")
        half_set = sem("half_set")
        sumsq, mean_ready, rstd_ready = sem("sumsq"), sem("mean_ready"), sem("rstd_ready")
        normed_ready, scaled_ready, res_ready = sem("normed_ready"), sem("scaled_ready"), sem("res_ready")
        xT_ready, xhi_ready, xlo_ready = sem("xT_ready"), sem("xhi_ready"), sem("xlo_ready")
        silu_ready, prod_ready, hhi_ready, hlo_ready = sem("silu_ready"), sem("prod_ready"), sem("hhi_ready"), sem("hlo_ready")
        ghi_ready, glo_ready = sem("ghi_ready"), sem("glo_ready")
        pre_mm, pre_evac = sem("pre_mm"), sem("pre_evac")
        vrev_out, skew_in = sem("vrev_out"), sem("skew_in")
        bias_mm, bias_ready = sem("bias_mm"), sem("bias_ready")
        proj_ready = sem("proj_ready")
        w1_in = [sem("w1k_in"), sem("w1v_in")]
        pairs_in = [sem("pairsk_in"), sem("pairsv_in")]
        kx_in = sem("kx_in")
        gates_mm, gate_exp, gate_step, gate_ready = sem("gates_mm"), sem("gate_exp"), sem("gate_step"), sem("gate_ready")
        flat_ready, hid_mm, hid_ready, hidR_zero, hidR_ready = sem("flat_ready"), sem("hid_mm"), sem("hid_ready"), sem("hidR_zero"), sem("hidR_ready")
        cmp_mm, cmp_ready = sem("cmp_mm"), sem("cmp_ready")
        sc_mm, sc_step, sc_logits, sc_exp = sem("sc_mm"), sem("sc_step"), sem("sc_logits"), sem("sc_exp")
        probc_zero, probc_ready, probcT_mm, probcT_ready = sem("probc_zero"), sem("probc_ready"), sem("probcT_mm"), sem("probcT_ready")
        scores_mm, logits_ready, exp_done = sem("scores_mm"), sem("logits_ready"), sem("exp_done")
        rsum_ready, fac_ready, prob_ready = sem("rsum_ready"), sem("fac_ready"), sem("prob_ready")
        probT_mm, probT_ready, heads_mm = sem("probT_mm"), sem("probT_ready"), sem("heads_mm")
        ohi_ready, olo_ready = sem("ohi_ready"), sem("olo_ready")
        fz_ready, fT_mm, f_step, f_exp, f_ln, cum_ready, decay_ready = (
            sem("fz_ready"), sem("fT_mm"), sem("f_step"), sem("f_exp"), sem("f_ln"), sem("cum_ready"), sem("decay_ready"))
        stored = sem("stored")

        STAGE0 = {"nsa": 0, "fox": H}
        PAIR0 = {"nsa": 0, "fox": 8}
        PROJ0 = {"nsa": 0, "fox": 10}
        STAGES = {"nsa": H, "fox": H // 2}

        def G_(u0, c):
            return u0 if isinstance(c, int) and c == 0 else u0 - 1 + 3 * c

        block = ctx.enter_context(nc.Block())

        @block.sync
        def _(sp):
            def load(u, uses, view, src):
                if not (isinstance(u, int) and u < RING):
                    sp.wait_ge(w_lo, u - RING + 1)
                dst = raw[:, view[0], :].rearrange("p (a n) -> p a n", a=view[1])
                sp.dma_start(dst, src).then_inc(raw_in[view[0]], 16)

            def load_cols(u, slot, w, c0):
                load(u, None, (slot, KT), w[:, bass.ds(c0, UC)].rearrange("(k p) n -> p k n", p=P))

            def load_rows(u, slot, w, r0):
                load(u, None, (slot, 2), w[bass.ds(r0, UC), :].rearrange("(k p) n -> p k n", p=P))

            for t in range(TT):
                sp.dma_start(res[:, t, :], x[0, t * P:(t + 1) * P, :]).then_inc(res_in, 16)
            for s, kind in enumerate(KINDS):
                u0 = U0[s]
                if kind == "ffn":
                    i, m = WHICH[s]
                    load_cols(u0, u0 % RING, w_gate[i, m], 0)
                    load_cols(u0 + 1, (u0 + 1) % RING, w_up[i, m], 0)
                    with sp.Fori(1, NCH) as c:
                        load_cols(u0 - 1 + 3 * c, (u0 + 2) % RING, w_gate[i, m], c * UC)
                        load_rows(u0 + 3 * c, u0 % RING, w_down[i, m], c * UC - UC)
                        load_cols(u0 + 1 + 3 * c, (u0 + 1) % RING, w_up[i, m], c * UC)
                    load_rows(u0 + 32, (u0 + 32) % RING, w_down[i, m], (NCH - 1) * UC)
                else:
                    w, wo = (nsa_in[0], nsa_out[0]) if kind == "nsa" else (fox_in[0], fox_out[0])
                    cols = [1024, 1280, 1536, 2048, 1792, 2304, 0, 256, 512, 768] if kind == "nsa" else [UC * k for k in range(12)]
                    for k, c0 in enumerate(cols):
                        load_cols(u0 + k, (u0 + k) % RING, w, c0)
                    for k in range(4):
                        u = u0 + len(cols) + k
                        load_rows(u, u % RING, wo, k * UC)
            for t in range(TT):
                sp.wait_ge(res_ready, TT * (NSUB - 1) + t + 1)
                sp.dma_start(out[0, t * P:(t + 1) * P, :], res[:, t, :]).then_inc(stored, 16)
            sp.wait_ge(stored, 16 * TT)

        @block.gpsimd
        def _(pool):
            def rstd_of(s, post):
                scale = 4.0 if post and KINDS[s] == "ffn" else 1.0
                for t in range(TT):
                    i = 4 * s + 2 * post + t
                    pool.wait_ge(sumsq, i + 1)
                    nc.gpsimd.tensor_scalar(ms[:, i:i + 1], ss[:, i:i + 1], scale / D, scale * EPS, ALU.mult, ALU.add).then_inc(mean_ready, 1)
                    pool.wait_ge(mean_ready, i + 1)
                    nc.gpsimd.tensor_tensor(rstd[:, i:i + 1], ms[:, i:i + 1], half[:, :], ALU.pow).then_inc(rstd_ready, 1)

            def load_gain(s, post):
                i, n = NORM[s]
                dst, signal = (g_post, gpost_in) if post else (g_pre, gpre_in)
                if s > 0:
                    pool.wait_ge(scaled_ready if post else normed_ready, TT * s)
                pool.dma_start(dst[:, :], bass.AP(norm_g.tensor, (i * 6 + n + post) * D, [[0, P], [1, D]])).then_inc(signal, 16)

            def scale_probs(n):
                b = n % 2
                pool.wait_ge(fac_ready, n + 1)
                for a in range(2):
                    for t, (c0, c1) in enumerate(((0, P), (P, SCORES))):
                        p_ = prob[:, b, a, c0:c1]
                        last = nc.gpsimd.tensor_scalar(p_, p_, fac[:, b, a, t:t + 1], 1.0, ALU.mult, ALU.mult)
                last.then_inc(prob_ready, 1)

            nc.gpsimd.memset(half[:, :], -0.5).then_inc(half_set, 1)
            load_gain(0, 0)
            pool.wait_ge(half_set, 1)
            rstd_of(0, 0)
            pool.wait_ge(pre_evac, 3)
            pool.dma_start(scratch, vrev[:, :]).then_inc(vrev_out, 16)
            pool.wait_ge(vrev_out, 16)
            pool.dma_start(skew, bass.AP(scratch.tensor, 0, [[1, P], [SCORES, H], [1, S]])).then_inc(skew_in, 16)
            load_gain(0, 1)
            load_gain(1, 0)
            pool.wait_ge(bias_mm, 8)
            pool.dma_start(w1, cmp_w1[0, 0].rearrange("(k p) n -> p k n", p=P)).then_inc(w1_in[0], 16)
            rstd_of(0, 1)
            rstd_of(1, 0)

            load_gain(1, 1)
            load_gain(2, 0)
            def pair_tokens(kv):
                pool.wait_ge(proj_ready, kv + 1)
                if kv:
                    pool.wait_ge(flat_ready, 1)
                for a in range(2):
                    src = kcv[64 * a:64 * a + 64, kv, :, :]
                    pool.dma_start(pairsv[0:64, a:G:2, :], src).then_inc(pairs_in[kv], 16)
                    pool.dma_start(pairsv[64:128, a:G:2, 0:S - 1], src[:, :, 1:S]).then_inc(pairs_in[kv], 16)

            pair_tokens(0)
            for r in range(2):
                pool.wait_ge(proj_ready, 3 + r)
                for a in range(2):
                    pool.dma_start(kX[64 * (1 - a):64 * (1 - a) + 64, r, :, :], kN[64 * a:64 * a + 64, r, :, :]).then_inc(kx_in, 16)
            pair_tokens(1)
            pool.wait_ge(hid_mm, 1)
            pool.dma_start(w1, cmp_w1[0, 1].rearrange("(k p) n -> p k n", p=P)).then_inc(w1_in[1], 16)
            nc.gpsimd.memset(probT_buf[:, 0:1024], 0.0).then_inc(hidR_zero, 1)
            pool.wait_ge(flat_ready, 2)
            nc.gpsimd.memset(pairs[:, :], 0.0).then_inc(probc_zero, 1)
            for n in range(H):
                scale_probs(n)
            rstd_of(1, 1)
            rstd_of(2, 0)
            for s in range(2, NSUB):
                load_gain(s, 1)
                if s + 1 < NSUB:
                    load_gain(s + 1, 0)
                if KINDS[s] == "fox":
                    pool.wait_ge(cum_ready, 1)
                    for h in range(H):
                        last = nc.gpsimd.tensor_scalar(bias[0:32, h, :], cum[:, :], cst[0:32, C_A1 + h:C_A1 + h + 1],
                                                       cst[0:32, C_A2 + h:C_A2 + h + 1], ALU.mult, ALU.add)
                    last.then_inc(decay_ready, 1)
                    for n in range(H, H + H // 2):
                        scale_probs(n)
                rstd_of(s, 1)
                if s + 1 < NSUB:
                    rstd_of(s + 1, 0)

        @block.scalar
        def _(act):
            def hi(u, slot, uses):
                act.wait_ge(raw_in[slot], 16 * uses)
                if not (isinstance(u, int) and u < RING):
                    act.wait_ge(unit_done, u - RING + 1)
                nc.scalar.activation(whi[:, slot, :], raw[:, slot, :], ACT.Copy).then_inc(w_hi, 1)

            def hi_static(u):
                if u < NUNITS:
                    hi(u, u % RING, u // RING + 1)

            def square(s, post):
                for t in range(TT):
                    i = 4 * s + 2 * post + t
                    if post:
                        src = ps[:, YB + 2 * t:YB + 2 * t + 2, :]
                        if t == 0:
                            act.wait_ge(unit_done, U0[s] + UNITS[KINDS[s]])
                            if KINDS[s] == "ffn":
                                act.wait_ge(hlo_ready, NCH * (FFN_OF[s] + 1))
                    else:
                        src = res[:, t, :].rearrange("p (a n) -> p a n", a=2)
                        act.wait_ge(res_in if s == 0 else res_ready, 16 * TT if s == 0 else TT * (s - 1) + t + 1)
                    if i >= 1:
                        act.wait_ge(sumsq, i)
                    nc.scalar.activation(ps[:, OB:OB + 2, :], src, ACT.Square, accum_out=ss[:, i:i + 1]).then_inc(sumsq, 1)

            def split_x(s):
                for t in range(TT):
                    for b in range(2):
                        i = 4 * s + 2 * t + b
                        act.wait_ge(xT_ready, i + 1)
                        src = ps[:, GB + 2 * t + b, :].rearrange("p (k n) -> p k n", k=4)
                        nc.scalar.activation(xhi[:, 4 * b:4 * b + 4, t * P:(t + 1) * P], src, ACT.Copy).then_inc(xhi_ready, 1)

            def silu(f, u0, c, first=False):
                act.wait_ge(unit_done, G_(u0, c) + 1)
                if not (isinstance(c, int) and c == 0 and f == 0):
                    act.wait_ge(prod_ready, NCH * f + c)
                nc.scalar.activation(silu_sb, ps[:, GB, :], ACT.Silu).then_inc(silu_ready, 1)

            def hidden_hi(f, c):
                act.wait_ge(prod_ready, NCH * f + c + 1)
                nc.scalar.activation(hhi[:, :, :], prod_sb.rearrange("p (a n) -> p a n", a=2), ACT.Copy).then_inc(hhi_ready, 1)

            def ffn(s):
                f, u0 = FFN_OF[s], U0[s]

                def chunk(c):
                    r = u0 // RING + c
                    dyn = not isinstance(c, int)

                    def split(k):
                        if dyn or u0 + 3 * c + k < NUNITS:
                            hi(u0 + k + 3 * c, (u0 + k) % RING, (u0 + k) // RING + 1 + c)
                    hidden_hi(f, c - 1)
                    split(1)
                    silu(f, u0, c)
                    split(2)
                    split(3)
                hi_static(u0 + 2)
                silu(f, u0, 0)
                hi_static(u0 + 3)
                chunk(1)
                if s == 0:
                    for k in range(8):
                        act.wait_ge(bias_mm, k + 1)
                        nc.scalar.activation(bias[:, 2 * k:2 * k + 2, :], ps[:, OB + k % 2, :].rearrange("p (a n) -> p a n", a=2),
                                             ACT.Copy).then_inc(bias_ready, 1)
                with act.Fori(2, NCH - 1) as c:
                    chunk(c)
                chunk(NCH - 1)
                hidden_hi(f, NCH - 1)
                hi_static(u0 + 34)

            def attend(kind):
                n0, p0, N = STAGE0[kind], PAIR0[kind], STAGES[kind]
                per = 2 if kind == "nsa" else 1

                def exps(n):
                    b = n % 2
                    act.wait_ge(logits_ready, n + 1)
                    for a in range(2):
                        for t, (c0, c1) in enumerate(((0, P), (P, SCORES))):
                            p_ = prob[:, b, a, c0:c1]
                            last = nc.scalar.activation(p_, p_, ACT.Exp, bias=nmax[:, b, a, t:t + 1], scale=-1.0,
                                                        accum_out=ssum[:, b, a, t:t + 1])
                    last.then_inc(exp_done, 1)

                def heads_hi(k):
                    act.wait_ge(heads_mm, n0 + per * (k + 1))
                    nc.scalar.activation(xhi[:, k, :], ps[:, OB + k % 2, 0:S], ACT.Copy).then_inc(ohi_ready, 1)
                for i in range(N + 4):
                    if i < N:
                        exps(n0 + i)
                    if i >= 4 and (i - 3) % per == 0:
                        heads_hi((i - 3) // per - 1)

            act.dma_start(cst[:, :], consts).then_inc(cst_in, 16)
            act.dma_start(pairs[0:NB + 1, 0:896], onehots).then_inc(oh_in, 16)
            act.dma_start(tab[0:NB, :], rel_bias).then_inc(tab_in, 16)
            act.dma_start(tab[NB:NB + 1, :], consts[NB:NB + 1, C_NEG:C_NEG + H]).then_inc(tab_in, 16)
            act.dma_start(small[0:32, :], cmp_pe[0].rearrange("v (k q) d -> (v k) (q d)", q=2)).then_inc(small_in, 16)
            act.dma_start(small[32:36, :], cmp_b1[0].rearrange("v (m q) -> (v m) q", q=P)).then_inc(small_in, 16)
            act.dma_start(gw[:, :, 0:48], nsa_in[0][:, 2560:2608].rearrange("(k p) n -> p k n", p=P)).then_inc(gw_in, 16)
            act.dma_start(gw[:, :, 48:64], fox_in[0][:, 3072:3088].rearrange("(k p) n -> p k n", p=P)).then_inc(gw_in, 16)
            for r in range(2):
                act.dma_start(w2k[:, :, r, :], cmp_w2[0, 0].rearrange("(m p) n -> p m n", p=P)).then_inc(w2_in, 16)
                act.dma_start(bf[16 * r:16 * r + 16, :], fox_bf[0].rearrange("(h a) -> h a", a=1)).then_inc(bf_in, 16)
            act.dma_start(w2v[:, :, :], cmp_w2[0, 1].rearrange("(m p) n -> p m n", p=P)).then_inc(w2_in, 16)

            square(0, 0)
            hi_static(0)
            hi_static(1)
            act.wait_ge(gw_in, 32)
            nc.scalar.activation(ghi[:, :, :], gw, ACT.Copy).then_inc(ghi_ready, 1)
            split_x(0)
            for s, kind in enumerate(KINDS):
                u0 = U0[s]
                if kind == "ffn":
                    ffn(s)
                else:
                    nproj = 10 if kind == "nsa" else 12

                    def evacuate(k):
                        act.wait_ge(unit_done, u0 + k + 1)
                        src = ps[:, GB + k % 2, :].rearrange("p (a n) -> p a n", a=2)
                        scale = 1.0
                        if kind == "nsa":
                            if k >= 6:
                                dst, scale = qT[:, 2 * (k - 6):2 * (k - 6) + 2, :], DH ** -0.5
                            else:
                                dst = [kcv[:, 0], kcv[:, 1], kN[:, 0], kN[:, 1], vN[:, 0], vN[:, 1]][k]
                        elif k < 4:
                            dst, scale = qT[:, 2 * k:2 * k + 2, :], DH ** -0.5
                        elif k < 8:
                            dst = kF[:, 2 * (k - 4):2 * (k - 4) + 2, :]
                        else:
                            dst = vF[:, :, (k - 8) * UC:(k - 7) * UC]
                        nc.scalar.activation(dst, src, ACT.Copy, scale=scale).then_inc(proj_ready, 1)
                    hi_static(u0 + 2)
                    for k in range(1, nproj):
                        evacuate(k - 1)
                        hi_static(u0 + k + 2)
                        if kind == "nsa" and k == 6:
                            act.wait_ge(gates_mm, 1)
                            nc.scalar.activation(gate_e[:, :, :], ps[:, OB, 0:96].rearrange("p (t n) -> p t n", t=TT),
                                                 ACT.Exp, scale=-1.0).then_inc(gate_exp, 1)
                        if kind == "nsa" and k == 8:
                            act.wait_ge(hid_mm, 1)
                            for m in range(2):
                                last = nc.scalar.activation(hid[:, m, :], ps[:, MB, m * 64:m * 64 + G * NC], ACT.Gelu_apprx_tanh,
                                                            bias=smallT[:, 32 + m:33 + m])
                            last.then_inc(hid_ready, 1)
                        if kind == "fox" and k == 1:
                            act.wait_ge(gates_mm, 2)
                            for r in range(2):
                                last = nc.scalar.activation(fz[:, :, 16 * r:16 * r + 16],
                                                            ps[:, OB, 0:32].rearrange("p (t n) -> p t n", t=TT), ACT.Copy)
                            last.then_inc(fz_ready, 1)
                        if kind == "fox" and k == 2:
                            act.wait_ge(f_step, 2)
                            nc.scalar.activation(fT[:, 2, :], fT[:, 1, :], ACT.Exp, scale=-1.0).then_inc(f_exp, 1)
                            act.wait_ge(f_exp, 1)
                            nc.scalar.activation(fT[:, 3, :], fT[:, 2, :], ACT.Ln, bias=1.0).then_inc(f_ln, 1)
                    evacuate(nproj - 1)
                    if kind == "nsa":
                        act.wait_ge(hid_mm, 2)
                        act.wait_ge(cmp_mm, 1)
                        for m in range(2):
                            last = nc.scalar.activation(hid[:, m, :], ps[:, MB, m * 64:m * 64 + G * NC], ACT.Gelu_apprx_tanh,
                                                        bias=smallT[:, 34 + m:35 + m])
                        last.then_inc(hid_ready, 1)
                        act.wait_ge(sc_logits, 1)
                        nc.scalar.activation(sc[:, :, :, :], sc[:, :, :, :], ACT.Exp).then_inc(sc_exp, 1)
                    attend(kind)
                    for k in range(4):
                        hi_static(u0 + nproj + k + 2)
                square(s, 1)
                if s + 1 < NSUB:
                    square(s + 1, 0)
                    split_x(s + 1)

        @block.vector
        def _(dve):
            def lo(u, slot):
                dve.wait_ge(w_hi, u + 1)
                nc.vector.tensor_tensor(wlo[:, slot, :], raw[:, slot, :], whi[:, slot, :].bitcast(F32), ALU.subtract).then_inc(w_lo, 1)

            def lo_static(u):
                if u < NUNITS:
                    lo(u, u % RING)

            def add_normed(s):
                dve.wait_ge(gpost_in, 16 * (s + 1))
                for t in range(TT):
                    i = 4 * s + 2 + t
                    dve.wait_ge(rstd_ready, i + 1)
                    for b in range(2):
                        last = nc.vector.scalar_tensor_tensor(normed[:, t, 512 * b:512 * b + 512], ps[:, YB + 2 * t + b, :], rstd[:, i:i + 1],
                                                              g_post[:, 512 * b:512 * b + 512], ALU.mult, ALU.mult)
                    last.then_inc(scaled_ready, 1)
                    dve.wait_ge(scaled_ready, TT * s + t + 1)
                    nc.vector.tensor_tensor(res[:, t, :], res[:, t, :], normed[:, t, :], ALU.add).then_inc(res_ready, 1)

            def norm_input(s):
                dve.wait_ge(gpre_in, 16 * (s + 1))
                for t in range(TT):
                    i = 4 * s + t
                    dve.wait_ge(rstd_ready, i + 1)
                    nc.vector.scalar_tensor_tensor(normed[:, t, :], res[:, t, :], rstd[:, i:i + 1], g_pre[:, :],
                                                   ALU.mult, ALU.mult).then_inc(normed_ready, 1)
                for t in range(TT):
                    for b in range(2):
                        dve.wait_ge(xhi_ready, 4 * s + 2 * t + b + 1)
                        src = ps[:, GB + 2 * t + b, :].rearrange("p (k n) -> p k n", k=4)
                        at = (slice(None), slice(4 * b, 4 * b + 4), slice(t * P, (t + 1) * P))
                        nc.vector.tensor_tensor(xlo[at], src, xhi[at].bitcast(F32), ALU.subtract).then_inc(xlo_ready, 1)

            def hidden(f, u0, c):
                dve.wait_ge(unit_done, (u0 + 2) if isinstance(c, int) and c == 0 else u0 + 2 + 3 * c)
                dve.wait_ge(silu_ready, NCH * f + c + 1)
                nc.vector.tensor_tensor(prod_sb, silu_sb, ps[:, UB, :], ALU.mult).then_inc(prod_ready, 1)
                dve.wait_ge(hhi_ready, NCH * f + c + 1)
                nc.vector.tensor_tensor(hlo[:, :, :], prod_sb.rearrange("p (a n) -> p a n", a=2), hhi[:, :, :].bitcast(F32),
                                        ALU.subtract).then_inc(hlo_ready, 1)

            def ffn(s):
                f, u0 = FFN_OF[s], U0[s]

                def chunk(c):
                    hidden(f, u0, c - 1)
                    for k in (1, 2, 3):
                        if not isinstance(c, int) or u0 + 3 * c + k < NUNITS:
                            lo(u0 + k + 3 * c, (u0 + k) % RING)
                lo_static(u0 + 2)
                lo_static(u0 + 3)
                chunk(1)
                with dve.Fori(2, NCH - 1) as c:
                    chunk(c)
                chunk(NCH - 1)
                hidden(f, u0, NCH - 1)
                lo_static(u0 + 34)

            def attend(kind):
                n0, p0, N = STAGE0[kind], PAIR0[kind], STAGES[kind]
                per = 2 if kind == "nsa" else 1
                mask = cst[:, C_MASK:C_MASK + S]

                def logits(n):
                    b = n % 2
                    dve.wait_ge(scores_mm, n + 1)
                    if n >= 2:
                        dve.wait_ge(probT_mm, n - 1)
                    for a in range(2):
                        for t, (c0, c1) in enumerate(((0, P), (P, SCORES))):
                            j0 = P if t == 0 else 0
                            add = bias[:, n, j0:S] if kind == "nsa" else mask[:, j0:S]
                            last = nc.vector.tensor_tensor_reduce(
                                out=prob[:, b, a, c0:c1], in0=ps[:, 2 * b + a, c0:c1], in1=add, scale=-1.0, scalar=3e38,
                                op0=ALU.add, op1=ALU.min, accum_out=nmax[:, b, a, t:t + 1])
                    last.then_inc(logits_ready, 1)

                def factors(n):
                    b = n % 2
                    dve.wait_ge(exp_done, n + 1)
                    if kind == "nsa":
                        nc.vector.reciprocal(rsum[:, b], ssum[:, b]).then_inc(rsum_ready, 1)
                        dve.wait_ge(rsum_ready, n + 1)
                        g_ = gate[:, :, 16 + n:48:16].rearrange("p t a -> p a t")
                        nc.vector.tensor_tensor(fac[:, b], rsum[:, b], g_, ALU.mult).then_inc(fac_ready, 1)
                    else:
                        nc.vector.reciprocal(fac[:, b], ssum[:, b]).then_inc(fac_ready, 1)

                def probs_T(n):
                    b = n % 2
                    dve.wait_ge(probT_mm, n + 1)
                    if n >= 2:
                        dve.wait_ge(heads_mm, n - 1)
                    nc.vector.tensor_copy(probT[:, b], ps[:, GB:GB + 2, 0:SCORES]).then_inc(probT_ready, 1)

                def heads_lo(k):
                    dve.wait_ge(ohi_ready, p0 + k + 1)
                    nc.vector.tensor_tensor(xlo[:, k, :], ps[:, OB + k % 2, 0:S], xhi[:, k, :].bitcast(F32),
                                            ALU.subtract).then_inc(olo_ready, 1)
                for i in range(N + 4):
                    if i < N:
                        logits(n0 + i)
                    if 2 <= i < N + 2:
                        probs_T(n0 + i - 2)
                    if 1 <= i < N + 1:
                        factors(n0 + i - 1)
                    if i >= 4 and (i - 3) % per == 0:
                        heads_lo((i - 3) // per - 1)

            dve.wait_ge(pre_mm, 1)
            nc.vector.tensor_copy(smallT[:, :], ps[:, YB, 0:36]).then_inc(pre_evac, 1)
            for t in range(TT):
                last = nc.vector.tensor_copy(biasc[:, t].rearrange("p h c -> p c h"),
                                             ps[:, YB + 1, t * 240:(t + 1) * 240].rearrange("p (c h) -> p c h", h=H))
            last.then_inc(pre_evac, 1)
            nc.vector.tensor_copy(vrev[:, :], ps[0:H, YB + 2, 0:SCORES]).then_inc(pre_evac, 1)
            norm_input(0)
            lo_static(0)
            lo_static(1)
            dve.wait_ge(ghi_ready, 1)
            nc.vector.tensor_tensor(glo[:, :, :], gw, ghi[:, :, :].bitcast(F32), ALU.subtract).then_inc(glo_ready, 1)
            for s, kind in enumerate(KINDS):
                u0 = U0[s]
                if kind == "ffn":
                    ffn(s)
                else:
                    nproj = 10 if kind == "nsa" else 12

                    def gather(kv):
                        dve.wait_ge(pairs_in[kv], 64)
                        if kv:
                            dve.wait_ge(hid_mm, 1)
                        src = pairsv[:, :, :]
                        src = bass.AP(pairs[:, :].tensor, pairs[:, :].offset, [list(pairs[:, :].ap[0]), [2, 16], [S, G], [CS, NC]])
                        pe_ = smallT[:, 16 * kv:16 * kv + 16]
                        pe_ = bass.AP(pe_.tensor, pe_.offset, [list(pe_.ap[0]), [1, 16], [0, G], [0, NC]])
                        dst = flat[:, 0:960].rearrange("p (k g c) -> p k g c", k=16, g=G)
                        nc.vector.tensor_tensor(dst, src, pe_, ALU.add).then_inc(flat_ready, 1)
                    lo_static(u0 + 2)
                    for k in range(1, nproj):
                        lo_static(u0 + k + 2)
                        if kind == "nsa":
                            if k == 6:
                                dve.wait_ge(gate_exp, 1)
                                nc.vector.tensor_scalar(gate_e[:, :, :], gate_e[:, :, :], 1.0, None, ALU.add).then_inc(gate_step, 1)
                                dve.wait_ge(gate_step, 1)
                                nc.vector.reciprocal(gate[:, :, :], gate_e[:, :, :]).then_inc(gate_ready, 1)
                            if k == 5:
                                gather(0)
                            if k == 8:
                                gather(1)
                                dve.wait_ge(cmp_mm, 1)
                                nc.vector.tensor_copy(kcmp[:, :], ps[:, MB, 128:128 + G * NC]).then_inc(cmp_ready, 1)
                        elif k == 2:
                            dve.wait_ge(fT_mm, 1)
                            dve.wait_ge(bf_in, 32)
                            nc.vector.tensor_scalar(fT[:, 0, :], ps[0:32, MB, 0:S], bf[:, :], None, ALU.add).then_inc(f_step, 1)
                            dve.wait_ge(f_step, 1)
                            nc.vector.scalar_tensor_tensor(fT[:, 1, :], fT[:, 0, :], -1.0, fT[:, 0, :], ALU.mult, ALU.max).then_inc(f_step, 1)
                        elif k == 3:
                            dve.wait_ge(f_ln, 1)
                            nc.vector.scalar_tensor_tensor(fT[:, 1, :], fT[:, 0, :], 0.0, fT[:, 3, :], ALU.min, ALU.subtract).then_inc(f_step, 1)
                            dve.wait_ge(f_step, 3)
                            nc.vector.memset(rhsd[:, :], 0.0).then_inc(f_step, 1)
                            dve.wait_ge(f_step, 4)
                            nc.vector.tensor_tensor_scan(cum[:, :], rhsd[:, :], fT[:, 1, :], 0.0, ALU.add, ALU.add).then_inc(cum_ready, 1)
                            dve.wait_ge(cum_ready, 1)
                            nc.vector.tensor_scalar(rhsd[:, :], cum[:, :], cst[0:32, C_R:C_R + 1], cst[0:32, C_R + 1:C_R + 2],
                                                    ALU.mult, ALU.add).then_inc(f_step, 1)
                    if kind == "nsa":
                        dve.wait_ge(hid_ready, 2)
                        dve.wait_ge(hidR_zero, 1)
                        for m in range(2):
                            src = hid[:, m, :]
                            src = bass.AP(src.tensor, src.offset, [list(src.ap[0]), [NC, G], [0, 4], [1, NC]])
                            last = nc.vector.tensor_copy(hidR[:, m, :, :, 0:NC], src)
                        last.then_inc(hidR_ready, 1)
                        dve.wait_ge(cmp_mm, 2)
                        nc.vector.tensor_copy(vcmp[:, :, :], ps[:, MB, 192:448].rearrange("p (g d) -> p g d", g=G)).then_inc(cmp_ready, 1)
                        dve.wait_ge(sc_mm, 1)
                        s3 = sc[:, :, :, :].rearrange("p t h c -> p (t h) c")
                        for r, bank in enumerate((OB, UB)):
                            last = nc.vector.tensor_tensor(sc[:, :, r:H:2, :], ps[:, bank, 0:240].rearrange("p (t h c) -> p t h c", t=TT, c=NC),
                                                           biasc[:, :, r:H:2, :], ALU.add)
                        last.then_inc(sc_step, 1)
                        dve.wait_ge(sc_step, 1)
                        nc.vector.tensor_reduce(cmx[:, :, :].rearrange("p t h -> p (t h)"), s3, AX.X, ALU.max).then_inc(sc_step, 1)
                        dve.wait_ge(sc_step, 2)
                        def spread(v):
                            return bass.AP(v[:, :, :].tensor, v[:, :, :].offset, [list(v[:, :, :].ap[0]), [1, TT * H], [0, NC]])
                        nc.vector.tensor_tensor(s3, s3, spread(cmx), ALU.subtract).then_inc(sc_logits, 1)
                        dve.wait_ge(sc_exp, 1)
                        nc.vector.tensor_reduce(csum[:, :, :].rearrange("p t h -> p (t h)"), s3, AX.X, ALU.add).then_inc(sc_step, 1)
                        dve.wait_ge(sc_step, 3)
                        nc.vector.reciprocal(cfac[:, :, :], csum[:, :, :]).then_inc(sc_step, 1)
                        dve.wait_ge(sc_step, 4)
                        for t in range(TT):
                            last = nc.vector.scalar_tensor_tensor(cfac[:, t, :], cfac[:, t, :], cst[:, C_VALID + t:C_VALID + t + 1],
                                                                  gate[:, t, 0:H], ALU.mult, ALU.mult)
                        last.then_inc(sc_step, 1)
                        dve.wait_ge(sc_step, 5)
                        dve.wait_ge(probc_zero, 1)
                        nc.vector.tensor_tensor(probc.rearrange("p t h c -> p (t h) c")[:, :, 0:NC], s3, spread(cfac), ALU.mult).then_inc(probc_ready, 1)
                        for t in range(TT):
                            dve.wait_ge(probcT_mm, t + 1)
                            nc.vector.tensor_copy(probcT[:, :, t * P:(t + 1) * P],
                                                  ps[:, MB - t, :].rearrange("p (g n) -> p g n", g=G)).then_inc(probcT_ready, 1)
                    attend(kind)
                    for k in range(4):
                        lo_static(u0 + nproj + k + 2)
                add_normed(s)
                if s + 1 < NSUB:
                    norm_input(s + 1)

        @block.tensor
        def _(pe):
            def mm(out_, l, r, start, stop):
                return nc.tensor.matmul(out_, l, r, start=start, stop=stop)

            def split_mm(out_, l, r, start, stop):
                (lh, ll), (rh, rl) = l, r
                mm(out_, lh, rh, start, False)
                mm(out_, lh, rl, False, False)
                return mm(out_, ll, rh, False, stop)

            def wcols(slot):
                return [w[:, slot, :].rearrange("p (k n) -> p k n", k=KT) for w in (whi, wlo)]

            def wrows(slot):
                return [w[:, slot, :].rearrange("p (k n) -> p k n", k=2) for w in (whi, wlo)]

            def features(u, slot, bank):
                pe.wait_ge(w_lo, u + 1)
                wh, wl = wcols(slot)
                for a in range(2):
                    for k in range(KT):
                        last = split_mm(ps[:, bank, a * S:(a + 1) * S], (wh[:, k, a * P:(a + 1) * P], wl[:, k, a * P:(a + 1) * P]),
                                        (xhi[:, k, :], xlo[:, k, :]), k == 0, k == KT - 1)
                last.then_inc(unit_done, 1)

            def tokens(u, slot, bank):
                pe.wait_ge(w_lo, u + 1)
                wh, wl = wcols(slot)
                for t in range(TT):
                    for k in range(KT):
                        last = split_mm(ps[:, bank, t * UC:(t + 1) * UC], (xhi[:, k, t * P:(t + 1) * P], xlo[:, k, t * P:(t + 1) * P]),
                                        (wh[:, k, :], wl[:, k, :]), k == 0, k == KT - 1)
                last.then_inc(unit_done, 1)

            def rows(u, slot, left, first, final):
                pe.wait_ge(w_lo, u + 1)
                wh, wl = wrows(slot)
                for k in range(2):
                    for t in range(TT):
                        for b in range(2):
                            l = [v[:, t * P:(t + 1) * P] for v in left(k)]
                            last = split_mm(ps[:, YB + 2 * t + b, :], l, (wh[:, k, 512 * b:512 * b + 512], wl[:, k, 512 * b:512 * b + 512]),
                                            first and k == 0, final and k == 1)
                last.then_inc(unit_done, 1)

            def transpose_input(s):
                for t in range(TT):
                    pe.wait_ge(normed_ready, TT * s + t + 1)
                    if t == 1:
                        pe.wait_ge(sumsq, 4 * s + 2)
                    for b in range(2):
                        for k in range(4):
                            last = nc.tensor.transpose(ps[:, GB + 2 * t + b, k * P:(k + 1) * P],
                                                       normed[:, t, (4 * b + k) * P:(4 * b + k + 1) * P], ident)
                        last.then_inc(xT_ready, 1)
                pe.wait_ge(xlo_ready, 4 * (s + 1))

            def ffn(s):
                f, u0 = FFN_OF[s], U0[s]

                def gate_(c, slot):
                    if not (isinstance(c, int) and c == 0):
                        pe.wait_ge(silu_ready, NCH * f + c)
                    features(G_(u0, c), slot, GB)

                def up_(c, slot):
                    if not (isinstance(c, int) and c == 0):
                        pe.wait_ge(prod_ready, NCH * f + c)
                    features((u0 + 1) if isinstance(c, int) and c == 0 else u0 + 1 + 3 * c, slot, UB)

                def down_(c, slot, first=False, final=False):
                    pe.wait_ge(hlo_ready, NCH * f + c + 1)
                    rows(u0 + 3 + 3 * c if not final else u0 + 32, slot, lambda k: (hhi[:, k, :], hlo[:, k, :]), first, final)

                def chunk(c, first=False):
                    gate_(c, (u0 + 2) % RING)
                    down_(c - 1, u0 % RING, first)
                    up_(c, (u0 + 1) % RING)
                gate_(0, u0 % RING)
                up_(0, (u0 + 1) % RING)
                chunk(1, True)
                if s == 0:
                    pe.wait_ge(skew_in, 16)
                    for k in range(8):
                        if k >= 2:
                            pe.wait_ge(bias_ready, k - 1)
                        mm(ps[:, OB + k % 2, :], cst[:, C_J:C_J + P], skew[:, 2 * k:2 * k + 2, :], True, True).then_inc(bias_mm, 1)
                with pe.Fori(2, NCH) as c:
                    chunk(c)
                down_(NCH - 1, (u0 + 32) % RING, False, True)

            def gates(n, c0, w):
                pe.wait_ge(glo_ready, 1)
                for t in range(TT):
                    for k in range(KT):
                        last = split_mm(ps[:, OB, t * w:(t + 1) * w], (xhi[:, k, t * P:(t + 1) * P], xlo[:, k, t * P:(t + 1) * P]),
                                        (ghi[:, k, c0:c0 + w], glo[:, k, c0:c0 + w]), k == 0, k == KT - 1)
                last.then_inc(gates_mm, 1)

            def compress(kv):
                pe.wait_ge(flat_ready, kv + 1)
                pe.wait_ge(w1_in[kv], 16)
                if kv:
                    pe.wait_ge(hid_ready, 1)
                    pe.wait_ge(cmp_ready, 1)
                for m in range(2):
                    for k in range(16):
                        last = mm(ps[:, MB, m * 64:m * 64 + G * NC], w1[:, k, m * P:(m + 1) * P], flatv[:, k, :], k == 0, k == 15)
                last.then_inc(hid_mm, 1)
                if kv == 0:
                    pe.wait_ge(w2_in, 48)
                    pe.wait_ge(hid_ready, 1)
                    for m in range(2):
                        last = mm(ps[:, MB, 128:128 + G * NC], w2k[:, m, :, :].rearrange("p r d -> p (r d)"), hid[:, m, :], m == 0, m == 1)
                else:
                    pe.wait_ge(hidR_ready, 1)
                    for g in range(G):
                        for m in range(2):
                            last = mm(ps[:, MB, 192 + g * DH:192 + (g + 1) * DH], hidR[:, m, g, :, :].rearrange("p r c -> p (r c)"),
                                      w2v[:, m, :], m == 0, m == 1)
                last.then_inc(cmp_mm, 1)

            def attend(kind, between=None):
                n0, p0, N = STAGE0[kind], PAIR0[kind], STAGES[kind]
                per = 2 if kind == "nsa" else 1

                def side(h):
                    return slice(64 * (h % 2), 64 * (h % 2) + 64)

                def keys(n, a):
                    if kind == "nsa":
                        h, g = n, n // G
                        k_ = kN if h % 2 == g % 2 else kX
                        return h, k_[side(h), a, g // 2, :]
                    h = 2 * (n - n0) + a
                    return h, kF[side(h), h // 2, :]

                def values(n, a, t):
                    if kind == "nsa":
                        return vN[:, a, t, (n // G) * DH:(n // G + 1) * DH]
                    h = 2 * (n - n0) + a
                    return vF[:, t, h * DH:(h + 1) * DH]

                def scores(n):
                    b = n % 2
                    if n >= 2:
                        pe.wait_ge(logits_ready, n - 1)
                    for a in range(2):
                        h, k_ = keys(n, a)
                        for t, (c0, c1) in enumerate(((0, P), (P, SCORES))):
                            o_ = ps[:, 2 * b + a, c0:c1]
                            last = mm(o_, qT[side(h), h // 2, t * P:(t + 1) * P], k_[:, 0:c1 - c0], True, kind == "nsa")
                            if kind == "fox":
                                last = mm(o_, bias[0:32, h, t * P:(t + 1) * P], rhsd[:, 0:c1 - c0], False, True)
                    last.then_inc(scores_mm, 1)

                def probs_T(n):
                    b = n % 2
                    pe.wait_ge(prob_ready, n + 1)
                    if n >= 1:
                        pe.wait_ge(probT_ready, n)
                    for a in range(2):
                        for k in range(3):
                            last = nc.tensor.transpose(ps[:, GB + a, k * P:(k + 1) * P], prob[:, b, a, k * P:(k + 1) * P], ident)
                    last.then_inc(probT_mm, 1)

                def heads(n):
                    b = n % 2
                    pe.wait_ge(probT_ready, n + 1)
                    pair = (n - n0) // per
                    if pair >= 2:
                        pe.wait_ge(olo_ready, p0 + pair - 1)
                    bank = OB + pair % 2
                    for a in range(2):
                        half_ = side(n) if kind == "nsa" else side(a)
                        start = kind == "fox" or a == 0
                        if kind == "nsa" and a == 0:
                            r = 32 * (n % G)
                            mm(ps[half_, bank, 0:S], vcmp[r:r + 32, n // G, :], probcT[r:r + 32, n // G, :], True, False)
                            start = False
                        mm(ps[half_, bank, 0:S], values(n, a, 0), probT[:, b, a, 0:S], start, False)
                        last = mm(ps[half_, bank, P:S], values(n, a, 1), probT[:, b, a, S:SCORES], False, kind == "fox" or a == 1)
                    last.then_inc(heads_mm, 1)
                for i in range(N + 3):
                    if i < N:
                        scores(n0 + i)
                    if between and i == 1:
                        between()
                    if 2 <= i < N + 2:
                        probs_T(n0 + i - 2)
                    if i >= 3:
                        heads(n0 + i - 3)

            pe.wait_ge(small_in, 32)
            pe.wait_ge(cst_in, 16)
            nc.tensor.transpose(ps[:, YB, 0:36], small[:, :], cst[0:36, C_ID:C_ID + 36])
            pe.wait_ge(tab_in, 32)
            pe.wait_ge(oh_in, 16)
            for t in range(TT):
                for c in range(NC):
                    m0 = t * P - (CS * c + CB - 1) + S
                    mm(ps[:, YB + 1, t * 240 + c * H:t * 240 + (c + 1) * H], near[:, m0:m0 + P], tab[:, :], True, True)
            mm(ps[0:H, YB + 2, 0:SCORES], tab[:, :], back, True, True).then_inc(pre_mm, 1)
            pe.wait_ge(pre_evac, 3)
            for s, kind in enumerate(KINDS):
                u0 = U0[s]
                transpose_input(s)
                if kind == "ffn":
                    ffn(s)
                    continue
                pr0 = PROJ0[kind]
                nproj = 10 if kind == "nsa" else 12
                for k in range(nproj):
                    if k >= 2:
                        pe.wait_ge(proj_ready, pr0 + k - 1)
                    by_token = k in (4, 5) if kind == "nsa" else k >= 8
                    (tokens if by_token else features)(u0 + k, (u0 + k) % RING, GB + k % 2)
                    if kind == "nsa" and k == 5:
                        gates(0, 0, 48)
                    if kind == "nsa" and k == 7:
                        compress(0)
                    if kind == "fox" and k == 0:
                        gates(1, 48, 16)
                    if kind == "fox" and k == 1:
                        pe.wait_ge(fz_ready, 1)
                        for t in range(TT):
                            last = nc.tensor.transpose(ps[0:32, MB, t * P:(t + 1) * P], fz[:, t, :], ident)
                        last.then_inc(fT_mm, 1)
                pe.wait_ge(proj_ready, pr0 + nproj)
                if kind == "nsa":
                    compress(1)
                    pe.wait_ge(gate_exp, 1)
                    for t in range(TT):
                        for h in range(H):
                            sd = slice(64 * (h % 2), 64 * (h % 2) + 64)
                            g = h // G
                            c0 = (t * H // 2 + h // 2) * NC
                            last = mm(ps[:, (OB, UB)[h % 2], c0:c0 + NC], qT[sd, h // 2, t * P:(t + 1) * P],
                                      kcmp[sd, g * NC:(g + 1) * NC], True, True)
                    last.then_inc(sc_mm, 1)
                    pe.wait_ge(kx_in, 64)

                    def compressed_T():
                        pe.wait_ge(probc_ready, 1)
                        pe.wait_ge(cmp_ready, 2)
                        for t in range(TT):
                            for g in range(G):
                                last = nc.tensor.transpose(ps[:, MB - t, g * P:(g + 1) * P],
                                                           probc[:, t, G * g:G * g + G, :].rearrange("p h c -> p (h c)"), ident)
                            last.then_inc(probcT_mm, 1)
                        pe.wait_ge(probcT_ready, 2)
                    attend(kind, compressed_T)
                else:
                    pe.wait_ge(decay_ready, 1)
                    pe.wait_ge(f_step, 5)
                    attend(kind)
                for k in range(4):
                    pe.wait_ge(olo_ready, PAIR0[kind] + 2 * k + 2)
                    u = u0 + nproj + k
                    rows(u, u % RING, lambda j: (xhi[:, 2 * k + j, :], xlo[:, 2 * k + j, :]), k == 0, k == 3)


_INS = ["x", "norm_g", "ffn_w_gate", "ffn_w_up", "ffn_w_down", "rel_bias", "nsa_w_in", "nsa_cmp_pe",
        "nsa_cmp_w1", "nsa_cmp_b1", "nsa_cmp_w2", "nsa_w_out", "fox_w_in", "fox_b_f", "fox_w_out"]


def kernel(**inputs):
    import concourse.bacc as _bacc
    from concourse.bass_utils import run_bass_kernel_spmd as _run

    nc = _bacc.Bacc("TRN2", target_bir_lowering=False, num_devices=1)
    arrays, args = {}, []
    consts, onehots = tables()
    for name, a in [(n, inputs[n]) for n in _INS] + [("consts", consts), ("onehots", onehots)]:
        a = np.ascontiguousarray(a)
        arrays[f"in_{name}"] = a
        args.append(nc.dram_tensor(f"in_{name}", a.shape, mybir.dt.from_np(a.dtype), kind="ExternalInput").ap())
    args.append(nc.dram_tensor("out_0", (1, S, D), F32, kind="ExternalOutput").ap())
    args.append(nc.dram_tensor("scratch", (H, SCORES), F32, kind="Internal").ap())
    trunk(nc, *args)
    r = _run(nc, [arrays], core_ids=[0])
    return r.results[0]["out_0"]
```

```python
from contextlib import ExitStack

import numpy as np

import concourse.bass as bass
from concourse import mybir

F32 = mybir.dt.float32
F32R = mybir.dt.float32r
ALU = mybir.AluOpType
ACT = mybir.ActivationFunctionType
AX = mybir.AxisListType

P = 128
D = 1024
S = 256
KT = D // P
TT = S // P
FF = 2816
UC = 256
NCH = FF // UC
H = 16
DH = 64
G = 4
CB, CS = 32, 16
NC = (S - CB) // CS + 1
CP = 32
HID = 256
NB = 32
NEG = -1e30
EPS = 1e-6
RING = 3
PB = 3
SCORES = S + P

KINDS = ["ffn", "nsa", "ffn", "ffn", "fox", "ffn"]
UNITS = {"ffn": 3 * NCH, "nsa": 14, "fox": 16}
U0 = [sum(UNITS[k] for k in KINDS[:s]) for s in range(len(KINDS))]
NUNITS = sum(UNITS[k] for k in KINDS)
NSUB = len(KINDS)
FFN_OF = {0: 0, 2: 1, 3: 2, 5: 3}
WHICH = [(0, 0), None, (0, 1), (1, 0), None, (1, 1)]
NORM = [(0, 0), (0, 2), (0, 4), (1, 0), (1, 2), (1, 4)]

C_ID, C_J, C_MASK, C_VALID, C_A1, C_A2, C_R, C_NEG = 0, 128, 256, 512, 514, 530, 546, 548
C_END = 564


def t5_bucket(rel):
    n = np.maximum(rel, 0)
    nf = np.maximum(n, 1).astype(np.float32)
    large = 16 + (np.log(nf / np.float32(16)) / np.float32(np.log(8.0)) * np.float32(16)).astype(np.int32)
    return np.where(n < 16, n, np.minimum(large, NB - 1))


def tables():
    c = np.zeros((P, C_END), np.float32)
    c[:, C_ID:C_ID + P] = np.eye(P)
    c[:, C_J:C_J + P] = np.eye(P)[::-1]
    p, j = np.arange(P)[:, None], np.arange(S)[None, :]
    c[:, C_MASK:C_MASK + S] = np.where(P + p - j >= 0, 0.0, NEG)
    for t in range(TT):
        c[:, C_VALID + t] = np.arange(P) + t * P >= CB - 1
    for h in range(H):
        c[h, C_A1 + h] = 1.0
        c[H + h, C_A2 + h] = 1.0
    c[H:2 * H, C_R] = -1.0
    c[0:H, C_R + 1] = 1.0
    c[NB, C_NEG:C_NEG + H] = NEG

    def onehot(rel):
        o = np.zeros((NB + 1, len(rel)), np.float32)
        o[np.where(rel < 0, NB, t5_bucket(rel)), np.arange(len(rel))] = 1.0
        return o

    near = onehot(np.arange(2 * S) - S)
    back = onehot(S - 1 - np.arange(S + P))
    return c, np.concatenate([near, back], 1)


def trunk(nc, x, norm_g, w_gate, w_up, w_down, rel_bias, nsa_in, cmp_pe, cmp_w1, cmp_b1, cmp_w2,
          nsa_out, fox_in, fox_bf, fox_out, consts, onehots, out, scratch):
    with ExitStack() as ctx:
        def sb(name, shape, dt=F32):
            return ctx.enter_context(nc.sbuf_tensor(name, shape, dt))

        def sem(name):
            return ctx.enter_context(nc.semaphore(name))

        raw = sb("raw", [P, RING, 2048])
        whi = sb("whi", [P, RING, 2048], F32R)
        wlo = sb("wlo", [P, RING, 2048], F32R)
        res = sb("res", [P, TT, D])
        xhi = sb("xhi", [P, KT, S], F32R)
        xlo = sb("xlo", [P, KT, S], F32R)
        hhi = sb("hhi", [P, 2, S], F32R)
        hlo = sb("hlo", [P, 2, S], F32R)
        work = sb("work", [P, 4 * SCORES])
        silu_sb = work[:, 0:512]
        prod_sb = work[:, 512:1024]
        g_pre = sb("g_pre", [P, D])
        g_post = sb("g_post", [P, D])
        normed = sb("normed", [P, TT, D])
        diag = sb("diag", [P, TT, P])
        prob = [v.rearrange("p (a n) -> p a n", a=2) for v in
                (work[:, 0:2 * SCORES], work[:, 2 * SCORES:4 * SCORES], normed[:, 0, 0:2 * SCORES])]
        big = sb("big", [P, 4096])
        skew = big[:, :].rearrange("p (h n) -> p h n", h=H)
        w1 = big[:, :].rearrange("p (k n) -> p k n", k=16)
        kF = big[:, 0:2048].rearrange("p (k n) -> p k n", k=KT)
        vF = big[:, 2048:4096].rearrange("p (t n) -> p t n", t=TT)
        bias = sb("bias", [P, H, S])
        kcv = work[:, 0:1024].rearrange("p (r g t) -> p r g t", r=2, g=2)
        kN = sb("kN", [P, 2, 2, S])
        kX = sb("kX", [P, 2, 2, S])
        vN = sb("vN", [P, 2, TT, S])
        qT = sb("qT", [P, KT, S])
        pairs = sb("pairs", [P, 1024])
        pairsv = pairs[:, :].rearrange("p (g t) -> p g t", g=G)
        probc = pairs[:, :].rearrange("p (t h c) -> p t h c", t=TT, h=H)
        near = pairs[0:NB + 1, 0:512]
        back = pairs[0:NB + 1, 512:896]
        flat = sb("flat", [P, 1024])
        flatv = flat[:, 0:16 * G * NC].rearrange("p (k n) -> p k n", k=16)
        gw = flat[:, 0:512].rearrange("p (k n) -> p k n", k=KT)
        probcT = flat[:, :].rearrange("p (g t) -> p g t", g=G)
        ghi = sb("ghi", [P, KT, DH], F32R)
        glo = sb("glo", [P, KT, DH], F32R)
        probT_buf = sb("probT_buf", [P, 4 * SCORES])
        probT = probT_buf[:, :].rearrange("p (b a n) -> p b a n", b=2, a=2)
        hidR = probT_buf[:, 0:1024].rearrange("p (m g r c) -> p m g r c", m=2, g=G, r=4)
        biasc = sb("biasc", [P, TT, H, NC])
        sc = sb("sc", [P, TT, H, NC])
        hid = sb("hid", [P, 2, G * NC])
        kcmp = sb("kcmp", [P, G * NC])
        vcmp = sb("vcmp", [P, G, DH])
        w2k = sb("w2k", [P, 2, 2, DH])
        w2v = sb("w2v", [P, 2, DH])
        cst = sb("cst", [P, C_END])
        tab = sb("tab", [NB + 1, H])
        small = sb("small", [36, P])
        smallT = sb("smallT", [P, 36])
        vrev = sb("vrev", [H, SCORES])
        gate_e = sb("gate_e", [P, TT, 48])
        gate = sb("gate", [P, TT, 48])
        fz = sb("fz", [P, TT, 32])
        fT = pairs[0:32, :].rearrange("p (k t) -> p k t", k=4)
        cum = flat[0:32, 0:S]
        rhsd = flat[0:32, S:2 * S]
        bf = sb("bf", [32, 1])
        ss = sb("ss", [P, 4 * NSUB])
        ms = sb("ms", [P, 4 * NSUB])
        rstd = sb("rstd", [P, 4 * NSUB])
        half = sb("half", [P, 1])
        nmax = sb("nmax", [P, PB, 2, TT])
        ssum = sb("ssum", [P, PB, 2, TT])
        rsum = sb("rsum", [P, PB, 2, TT])
        fac = sb("fac", [P, PB, 2, TT])
        cmx = sb("cmx", [P, TT, H])
        csum = sb("csum", [P, TT, H])
        cfac = sb("cfac", [P, TT, H])
        ps = ctx.enter_context(nc.psum_tensor("ps", [P, 8, 512], F32))
        ident = cst[:, C_ID:C_ID + P]
        YB, GB, UB, OB, MB = 0, 4, 5, 6, 7

        raw_in = [sem(f"raw_in{i}") for i in range(RING)]
        w_hi, w_lo, unit_done = sem("w_hi"), sem("w_lo"), sem("unit_done")
        res_in = [sem("res0_in"), sem("res1_in")]
        cst_in, gw_in, small_in = sem("cst_in"), sem("gw_in"), sem("small_in")
        tab_in, oh_in, w2_in, bf_in = sem("tab_in"), sem("oh_in"), sem("w2_in"), sem("bf_in")
        gpre_in, gpost_in = sem("gpre_in"), sem("gpost_in")
        half_set = sem("half_set")
        sumsq, mean_ready, rstd_ready = sem("sumsq"), sem("mean_ready"), sem("rstd_ready")
        y_ready, yg_ready, res_ready, normed_ready, diag_ready = (
            sem("y_ready"), sem("yg_ready"), sem("res_ready"), sem("normed_ready"), sem("diag_ready"))
        xT_ready, xhi_ready, xlo_ready = sem("xT_ready"), sem("xhi_ready"), sem("xlo_ready")
        silu_ready, prod_ready, hhi_ready, hlo_ready = sem("silu_ready"), sem("prod_ready"), sem("hhi_ready"), sem("hlo_ready")
        prodT_mm = sem("prodT_mm")
        ghi_ready, glo_ready = sem("ghi_ready"), sem("glo_ready")
        pre_mm, pre_evac = sem("pre_mm"), sem("pre_evac")
        vrev_out, skew_in = sem("vrev_out"), sem("skew_in")
        bias_mm, bias_ready = sem("bias_mm"), sem("bias_ready")
        proj_ready = sem("proj_ready")
        w1_in = [sem("w1k_in"), sem("w1v_in")]
        pairs_in = [sem("pairsk_in"), sem("pairsv_in")]
        kx_in = sem("kx_in")
        gates_mm, gate_exp, gate_step, gate_ready = sem("gates_mm"), sem("gate_exp"), sem("gate_step"), sem("gate_ready")
        flat_ready, hid_mm, hid_ready, hidR_zero, hidR_ready = sem("flat_ready"), sem("hid_mm"), sem("hid_ready"), sem("hidR_zero"), sem("hidR_ready")
        cmp_mm, cmp_ready = sem("cmp_mm"), sem("cmp_ready")
        sc_mm, sc_step, sc_logits, sc_exp = sem("sc_mm"), sem("sc_step"), sem("sc_logits"), sem("sc_exp")
        probc_zero, probc_ready, probcT_mm, probcT_ready = sem("probc_zero"), sem("probc_ready"), sem("probcT_mm"), sem("probcT_ready")
        scores_mm, logits_ready, exp_done = sem("scores_mm"), sem("logits_ready"), sem("exp_done")
        rsum_ready, fac_ready, prob_ready = sem("rsum_ready"), sem("fac_ready"), sem("prob_ready")
        probT_mm, probT_ready, heads_mm = sem("probT_mm"), sem("probT_ready"), sem("heads_mm")
        ohi_ready, olo_ready = sem("ohi_ready"), sem("olo_ready")
        fz_ready, fT_mm, f_step, f_exp, f_ln, cum_ready, decay_ready = (
            sem("fz_ready"), sem("fT_mm"), sem("f_step"), sem("f_exp"), sem("f_ln"), sem("cum_ready"), sem("decay_ready"))
        stored = sem("stored")

        STAGE0 = {"nsa": 0, "fox": H}
        PAIR0 = {"nsa": 0, "fox": 8}
        PROJ0 = {"nsa": 0, "fox": 10}
        STAGES = {"nsa": H, "fox": H // 2}

        def G_(u0, c):
            return u0 if isinstance(c, int) and c == 0 else u0 - 1 + 3 * c

        def wait_output(engine, s, t):
            if t == 0:
                engine.wait_ge(y_ready, s + 1)
            else:
                engine.wait_ge(unit_done, U0[s] + UNITS[KINDS[s]])

        block = ctx.enter_context(nc.Block())

        @block.sync
        def _(sp):
            def load(u, uses, view, src):
                if not (isinstance(u, int) and u < RING):
                    sp.wait_ge(w_lo, u - RING + 1)
                dst = raw[:, view[0], :].rearrange("p (a n) -> p a n", a=view[1])
                sp.dma_start(dst, src).then_inc(raw_in[view[0]], 16)

            def load_cols(u, slot, w, c0):
                load(u, None, (slot, KT), w[:, bass.ds(c0, UC)].rearrange("(k p) n -> p k n", p=P))

            def load_rows(u, slot, w, r0):
                load(u, None, (slot, 2), w[bass.ds(r0, UC), :].rearrange("(k p) n -> p k n", p=P))

            for t in range(TT):
                sp.dma_start(res[:, t, :], x[0, t * P:(t + 1) * P, :]).then_inc(res_in[t], 16)
            for s, kind in enumerate(KINDS):
                u0 = U0[s]
                if kind == "ffn":
                    i, m = WHICH[s]
                    load_cols(u0, u0 % RING, w_gate[i, m], 0)
                    load_cols(u0 + 1, (u0 + 1) % RING, w_up[i, m], 0)
                    with sp.Fori(1, NCH - 1) as c:
                        load_cols(u0 - 1 + 3 * c, (u0 + 2) % RING, w_gate[i, m], c * UC)
                        load_rows(u0 + 3 * c, u0 % RING, w_down[i, m], c * UC - UC)
                        load_cols(u0 + 1 + 3 * c, (u0 + 1) % RING, w_up[i, m], c * UC)
                    load_cols(u0 + 29, (u0 + 29) % RING, w_gate[i, m], (NCH - 1) * UC)
                    load_cols(u0 + 30, (u0 + 30) % RING, w_up[i, m], (NCH - 1) * UC)
                    load_rows(u0 + 31, (u0 + 31) % RING, w_down[i, m], (NCH - 2) * UC)
                    load_rows(u0 + 32, (u0 + 32) % RING, w_down[i, m], (NCH - 1) * UC)
                else:
                    w, wo = (nsa_in[0], nsa_out[0]) if kind == "nsa" else (fox_in[0], fox_out[0])
                    cols = [1792, 2304, 1024, 1280, 1536, 2048, 0, 256, 512, 768] if kind == "nsa" else [UC * k for k in (8, 9, 10, 11, 0, 1, 2, 3, 4, 5, 6, 7)]
                    for k, c0 in enumerate(cols):
                        load_cols(u0 + k, (u0 + k) % RING, w, c0)
                    for k in range(4):
                        u = u0 + len(cols) + k
                        load_rows(u, u % RING, wo, k * UC)
            for t in range(TT):
                sp.wait_ge(res_ready, TT * (NSUB - 1) + t + 1)
                sp.dma_start(out[0, t * P:(t + 1) * P, :], res[:, t, :]).then_inc(stored, 16)
            sp.wait_ge(stored, 16 * TT)

        @block.gpsimd
        def _(pool):
            def rstd_of(s, post):
                scale = 4.0 if post and KINDS[s] == "ffn" else 1.0
                for t in range(TT):
                    i = 4 * s + 2 * post + t
                    pool.wait_ge(sumsq, i + 1)
                    nc.gpsimd.tensor_scalar(ms[:, i:i + 1], ss[:, i:i + 1], scale / D, scale * EPS, ALU.mult, ALU.add).then_inc(mean_ready, 1)
                    pool.wait_ge(mean_ready, i + 1)
                    nc.gpsimd.tensor_tensor(rstd[:, i:i + 1], ms[:, i:i + 1], half[:, :], ALU.pow).then_inc(rstd_ready, 1)
                    if not post:
                        pool.wait_ge(rstd_ready, i + 1)
                        if s > 0:
                            pool.wait_ge(xT_ready, 4 * (s - 1) + 2 * t + 2)
                        nc.gpsimd.tensor_scalar(diag[:, t, :], ident, rstd[:, i:i + 1], 1.0, ALU.mult, ALU.mult).then_inc(diag_ready, 1)

            def load_gain(s, post):
                i, n = NORM[s]
                dst, signal = (g_post, gpost_in) if post else (g_pre, gpre_in)
                if s > 0:
                    pool.wait_ge(yg_ready if post else normed_ready, TT * s)
                pool.dma_start(dst[:, :], bass.AP(norm_g.tensor, (i * 6 + n + post) * D, [[0, P], [1, D]])).then_inc(signal, 16)

            def scale_probs(n):
                b = n % PB
                pool.wait_ge(fac_ready, n + 1)
                for a in range(2):
                    for t, (c0, c1) in enumerate(((0, P), (P, SCORES))):
                        p_ = prob[b][:, a, c0:c1]
                        last = nc.gpsimd.tensor_scalar(p_, p_, fac[:, b, a, t:t + 1], 1.0, ALU.mult, ALU.mult)
                last.then_inc(prob_ready, 1)

            nc.gpsimd.memset(half[:, :], -0.5).then_inc(half_set, 1)
            load_gain(0, 0)
            pool.wait_ge(half_set, 1)
            pool.wait_ge(cst_in, 16)
            rstd_of(0, 0)
            pool.wait_ge(pre_evac, 1)
            pool.dma_start(scratch, vrev[:, :]).then_inc(vrev_out, 16)
            pool.wait_ge(vrev_out, 16)
            pool.dma_start(skew, bass.AP(scratch.tensor, 0, [[1, P], [SCORES, H], [1, S]])).then_inc(skew_in, 16)
            load_gain(0, 1)
            load_gain(1, 0)
            pool.wait_ge(bias_mm, 8)
            pool.dma_start(w1, cmp_w1[0, 0].rearrange("(k p) n -> p k n", p=P)).then_inc(w1_in[0], 16)
            rstd_of(0, 1)
            rstd_of(1, 0)

            load_gain(1, 1)
            load_gain(2, 0)
            def pair_tokens(kv):
                pool.wait_ge(proj_ready, kv + 3)
                if kv:
                    pool.wait_ge(flat_ready, 1)
                for a in range(2):
                    src = kcv[64 * a:64 * a + 64, kv, :, :]
                    pool.dma_start(pairsv[0:64, a:G:2, :], src).then_inc(pairs_in[kv], 16)
                    pool.dma_start(pairsv[64:128, a:G:2, 0:S - 1], src[:, :, 1:S]).then_inc(pairs_in[kv], 16)

            pair_tokens(0)
            for r in range(2):
                pool.wait_ge(proj_ready, 5 + r)
                for a in range(2):
                    pool.dma_start(kX[64 * (1 - a):64 * (1 - a) + 64, r, :, :], kN[64 * a:64 * a + 64, r, :, :]).then_inc(kx_in, 16)
            pair_tokens(1)
            pool.wait_ge(hid_mm, 1)
            pool.dma_start(w1, cmp_w1[0, 1].rearrange("(k p) n -> p k n", p=P)).then_inc(w1_in[1], 16)
            nc.gpsimd.memset(probT_buf[:, 0:1024], 0.0).then_inc(hidR_zero, 1)
            pool.wait_ge(flat_ready, 2)
            nc.gpsimd.memset(pairs[:, :], 0.0).then_inc(probc_zero, 1)
            for n in range(H):
                scale_probs(n)
            rstd_of(1, 1)
            rstd_of(2, 0)
            for s in range(2, NSUB):
                load_gain(s, 1)
                if s + 1 < NSUB:
                    load_gain(s + 1, 0)
                if KINDS[s] == "fox":
                    pool.wait_ge(cum_ready, 1)
                    for h in range(H):
                        last = nc.gpsimd.tensor_scalar(bias[0:32, h, :], cum[:, :], cst[0:32, C_A1 + h:C_A1 + h + 1],
                                                       cst[0:32, C_A2 + h:C_A2 + h + 1], ALU.mult, ALU.add)
                    last.then_inc(decay_ready, 1)
                    for n in range(H, H + H // 2):
                        scale_probs(n)
                rstd_of(s, 1)
                if s + 1 < NSUB:
                    rstd_of(s + 1, 0)

        @block.scalar
        def _(act):
            def hi(u, slot, uses):
                act.wait_ge(raw_in[slot], 16 * uses)
                if not (isinstance(u, int) and u < RING):
                    act.wait_ge(unit_done, u - RING + 1)
                nc.scalar.activation(whi[:, slot, :], raw[:, slot, :], ACT.Copy).then_inc(w_hi, 1)

            def hi_static(u):
                if u < NUNITS:
                    hi(u, u % RING, u // RING + 1)

            def square(s, post, t):
                i = 4 * s + 2 * post + t
                if post:
                    src = ps[:, YB + 2 * t:YB + 2 * t + 2, :]
                    wait_output(act, s, t)
                else:
                    src = res[:, t, :].rearrange("p (a n) -> p a n", a=2)
                    act.wait_ge(res_in[t] if s == 0 else res_ready, 16 if s == 0 else TT * (s - 1) + t + 1)
                if i >= 1:
                    act.wait_ge(sumsq, i)
                nc.scalar.activation(ps[:, OB:OB + 2, :], src, ACT.Square, accum_out=ss[:, i:i + 1]).then_inc(sumsq, 1)

            def split_x(s, t):
                for b in range(2):
                    i = 4 * s + 2 * t + b
                    act.wait_ge(xT_ready, i + 1)
                    src = ps[:, GB + 2 * t + b, :].rearrange("p (k n) -> p k n", k=4)
                    nc.scalar.activation(xhi[:, 4 * b:4 * b + 4, t * P:(t + 1) * P], src, ACT.Copy).then_inc(xhi_ready, 1)

            def silu(f, u0, c, first=False):
                act.wait_ge(unit_done, G_(u0, c) + 1)
                if not (isinstance(c, int) and c == 0 and f == 0):
                    act.wait_ge(prod_ready, NCH * f + c)
                nc.scalar.activation(silu_sb, ps[:, GB, :], ACT.Silu).then_inc(silu_ready, 1)

            def hidden_hi(f, c, dst=hhi):
                if isinstance(c, int) and c == 0:
                    act.wait_ge(prodT_mm, f + 1)
                    src = ps[:, MB, :]
                else:
                    act.wait_ge(prod_ready, NCH * f + c + 1)
                    src = prod_sb
                nc.scalar.activation(dst[:, 0:2, :], src.rearrange("p (a n) -> p a n", a=2), ACT.Copy).then_inc(hhi_ready, 1)

            def ffn(s):
                f, u0 = FFN_OF[s], U0[s]

                def chunk(c):
                    r = u0 // RING + c
                    dyn = not isinstance(c, int)

                    def split(k):
                        if dyn or u0 + 3 * c + k < NUNITS:
                            hi(u0 + k + 3 * c, (u0 + k) % RING, (u0 + k) // RING + 1 + c)
                    hidden_hi(f, c - 1)
                    split(1)
                    silu(f, u0, c)
                    split(2)
                    split(3)
                hi_static(u0 + 2)
                silu(f, u0, 0)
                hi_static(u0 + 3)
                chunk(1)
                if s == 0:
                    act.wait_ge(gw_in, 32)
                    nc.scalar.activation(ghi[:, :, :], gw, ACT.Copy).then_inc(ghi_ready, 1)
                    chunk(2)
                    chunk(3)
                    for k in range(8):
                        act.wait_ge(bias_mm, k + 1)
                        nc.scalar.activation(bias[:, 2 * k:2 * k + 2, :], ps[:, OB + k % 2, :].rearrange("p (a n) -> p a n", a=2),
                                             ACT.Copy).then_inc(bias_ready, 1)
                with act.Fori(4 if s == 0 else 2, NCH - 1) as c:
                    chunk(c)
                hidden_hi(f, NCH - 2)
                hi_static(u0 + 31)
                silu(f, u0, NCH - 1)
                hi_static(u0 + 32)
                hidden_hi(f, NCH - 1, xhi)
                hi_static(u0 + 33)
                hi_static(u0 + 34)

            def attend(kind):
                n0, p0, N = STAGE0[kind], PAIR0[kind], STAGES[kind]
                per = 2 if kind == "nsa" else 1

                def exps(n):
                    b = n % PB
                    act.wait_ge(logits_ready, n + 1)
                    for a in range(2):
                        for t, (c0, c1) in enumerate(((0, P), (P, SCORES))):
                            p_ = prob[b][:, a, c0:c1]
                            last = nc.scalar.activation(p_, p_, ACT.Exp, bias=nmax[:, b, a, t:t + 1], scale=-1.0,
                                                        accum_out=ssum[:, b, a, t:t + 1])
                    last.then_inc(exp_done, 1)

                def heads_hi(k):
                    act.wait_ge(heads_mm, n0 + per * (k + 1))
                    nc.scalar.activation(xhi[:, k, :], ps[:, OB + k % 2, 0:S], ACT.Copy).then_inc(ohi_ready, 1)
                for i in range(N + 4):
                    if i < N:
                        exps(n0 + i)
                    if i >= 4 and (i - 3) % per == 0:
                        heads_hi((i - 3) // per - 1)

            act.dma_start(cst[:, :], consts).then_inc(cst_in, 16)
            act.dma_start(pairs[0:NB + 1, 0:896], onehots).then_inc(oh_in, 16)
            act.dma_start(tab[0:NB, :], rel_bias).then_inc(tab_in, 16)
            act.dma_start(tab[NB:NB + 1, :], consts[NB:NB + 1, C_NEG:C_NEG + H]).then_inc(tab_in, 16)
            act.dma_start(small[0:32, :], cmp_pe[0].rearrange("v (k q) d -> (v k) (q d)", q=2)).then_inc(small_in, 16)
            act.dma_start(small[32:36, :], cmp_b1[0].rearrange("v (m q) -> (v m) q", q=P)).then_inc(small_in, 16)
            act.dma_start(gw[:, :, 0:48], nsa_in[0][:, 2560:2608].rearrange("(k p) n -> p k n", p=P)).then_inc(gw_in, 16)
            act.dma_start(gw[:, :, 48:64], fox_in[0][:, 3072:3088].rearrange("(k p) n -> p k n", p=P)).then_inc(gw_in, 16)
            for r in range(2):
                act.dma_start(w2k[:, :, r, :], cmp_w2[0, 0].rearrange("(m p) n -> p m n", p=P)).then_inc(w2_in, 16)
                act.dma_start(bf[16 * r:16 * r + 16, :], fox_bf[0].rearrange("(h a) -> h a", a=1)).then_inc(bf_in, 16)
            act.dma_start(w2v[:, :, :], cmp_w2[0, 1].rearrange("(m p) n -> p m n", p=P)).then_inc(w2_in, 16)

            square(0, 0, 0)
            square(0, 0, 1)
            hi_static(0)
            split_x(0, 0)
            hi_static(1)
            split_x(0, 1)
            for s, kind in enumerate(KINDS):
                u0 = U0[s]
                if kind == "ffn":
                    ffn(s)
                else:
                    nproj = 10 if kind == "nsa" else 12

                    def evacuate(k):
                        act.wait_ge(unit_done, u0 + k + 1)
                        src = ps[:, GB + k % 2, :].rearrange("p (a n) -> p a n", a=2)
                        scale = 1.0
                        if kind == "nsa":
                            if k >= 6:
                                dst, scale = qT[:, 2 * (k - 6):2 * (k - 6) + 2, :], DH ** -0.5
                            else:
                                dst = [vN[:, 0], vN[:, 1], kcv[:, 0], kcv[:, 1], kN[:, 0], kN[:, 1]][k]
                        elif k < 4:
                            dst = vF[:, :, k * UC:(k + 1) * UC]
                        elif k < 8:
                            dst, scale = qT[:, 2 * (k - 4):2 * (k - 4) + 2, :], DH ** -0.5
                        else:
                            dst = kF[:, 2 * (k - 8):2 * (k - 8) + 2, :]
                        nc.scalar.activation(dst, src, ACT.Copy, scale=scale).then_inc(proj_ready, 1)
                    hi_static(u0 + 2)
                    for k in range(1, nproj):
                        evacuate(k - 1)
                        hi_static(u0 + k + 2)
                        if kind == "nsa" and k == 3:
                            act.wait_ge(gates_mm, 1)
                            nc.scalar.activation(gate_e[:, :, :], ps[:, OB, 0:96].rearrange("p (t n) -> p t n", t=TT),
                                                 ACT.Exp, scale=-1.0).then_inc(gate_exp, 1)
                        if kind == "nsa" and k in (6, 9):
                            kv = (k - 6) // 3
                            act.wait_ge(hid_mm, kv + 1)
                            if kv:
                                act.wait_ge(cmp_mm, 1)
                            for m in range(2):
                                last = nc.scalar.activation(hid[:, m, :], ps[:, MB, m * 64:m * 64 + G * NC], ACT.Gelu_apprx_tanh,
                                                            bias=smallT[:, 32 + 2 * kv + m:33 + 2 * kv + m])
                            last.then_inc(hid_ready, 1)
                        if kind == "fox" and k == 2:
                            act.wait_ge(gates_mm, 2)
                            for r in range(2):
                                last = nc.scalar.activation(fz[:, :, 16 * r:16 * r + 16],
                                                            ps[:, OB, 0:32].rearrange("p (t n) -> p t n", t=TT), ACT.Copy)
                            last.then_inc(fz_ready, 1)
                        if kind == "fox" and k == 3:
                            act.wait_ge(f_step, 2)
                            nc.scalar.activation(fT[:, 2, :], fT[:, 1, :], ACT.Exp, scale=-1.0).then_inc(f_exp, 1)
                            act.wait_ge(f_exp, 1)
                            nc.scalar.activation(fT[:, 3, :], fT[:, 2, :], ACT.Ln, bias=1.0).then_inc(f_ln, 1)
                    evacuate(nproj - 1)
                    if kind == "nsa":
                        act.wait_ge(sc_logits, 1)
                        nc.scalar.activation(sc[:, :, :, :], sc[:, :, :, :], ACT.Exp).then_inc(sc_exp, 1)
                    attend(kind)
                    for k in range(4):
                        hi_static(u0 + nproj + k + 2)
                square(s, 1, 0)
                square(s, 1, 1)
                if s + 1 < NSUB:
                    square(s + 1, 0, 0)
                    split_x(s + 1, 0)
                    square(s + 1, 0, 1)
                    split_x(s + 1, 1)

        @block.vector
        def _(dve):
            def lo(u, slot):
                dve.wait_ge(w_hi, u + 1)
                nc.vector.tensor_tensor(wlo[:, slot, :], raw[:, slot, :], whi[:, slot, :].bitcast(F32), ALU.subtract).then_inc(w_lo, 1)

            def lo_static(u):
                if u < NUNITS:
                    lo(u, u % RING)

            def gain_output(s, t):
                if t == 0:
                    dve.wait_ge(gpost_in, 16 * (s + 1))
                wait_output(dve, s, t)
                dve.wait_ge(sumsq, 4 * s + 3 + t)
                nc.vector.tensor_tensor(normed[:, t, :].rearrange("p (a n) -> p a n", a=2), ps[:, YB + 2 * t:YB + 2 * t + 2, :],
                                        g_post[:, :].rearrange("p (a n) -> p a n", a=2), ALU.mult).then_inc(yg_ready, 1)

            def add_output(s, t):
                i = 4 * s + 2 + t
                dve.wait_ge(yg_ready, TT * s + t + 1)
                dve.wait_ge(rstd_ready, i + 1)
                nc.vector.scalar_tensor_tensor(res[:, t, :], normed[:, t, :], rstd[:, i:i + 1], res[:, t, :],
                                               ALU.mult, ALU.add).then_inc(res_ready, 1)

            def gain_input(s, t):
                if t == 0:
                    dve.wait_ge(gpre_in, 16 * (s + 1))
                dve.wait_ge(res_in[t] if s == 0 else res_ready, 16 if s == 0 else TT * (s - 1) + t + 1)
                nc.vector.tensor_tensor(normed[:, t, :], res[:, t, :], g_pre[:, :], ALU.mult).then_inc(normed_ready, 1)

            def split_x(s, t):
                for b in range(2):
                    dve.wait_ge(xhi_ready, 4 * s + 2 * t + b + 1)
                    src = ps[:, GB + 2 * t + b, :].rearrange("p (k n) -> p k n", k=4)
                    at = (slice(None), slice(4 * b, 4 * b + 4), slice(t * P, (t + 1) * P))
                    nc.vector.tensor_tensor(xlo[at], src, xhi[at].bitcast(F32), ALU.subtract).then_inc(xlo_ready, 1)

            def hidden(f, u0, c, hi_=hhi, lo_=hlo, done=None):
                dve.wait_ge(unit_done, done or u0 + 2 + 3 * c)
                dve.wait_ge(silu_ready, NCH * f + c + 1)
                if not (isinstance(c, int) and c == 0 and f == 0):
                    dve.wait_ge(hlo_ready, NCH * f + c)
                nc.vector.tensor_tensor(prod_sb, silu_sb, ps[:, UB, :], ALU.mult).then_inc(prod_ready, 1)
                dve.wait_ge(hhi_ready, NCH * f + c + 1)
                src = ps[:, MB, :] if isinstance(c, int) and c == 0 else prod_sb
                nc.vector.tensor_tensor(lo_[:, 0:2, :], src.rearrange("p (a n) -> p a n", a=2), hi_[:, 0:2, :].bitcast(F32),
                                        ALU.subtract).then_inc(hlo_ready, 1)

            def ffn(s):
                f, u0 = FFN_OF[s], U0[s]

                def chunk(c):
                    hidden(f, u0, c - 1)
                    for k in (1, 2, 3):
                        if not isinstance(c, int) or u0 + 3 * c + k < NUNITS:
                            lo(u0 + k + 3 * c, (u0 + k) % RING)
                lo_static(u0 + 2)
                lo_static(u0 + 3)
                chunk(1)
                if s == 0:
                    dve.wait_ge(ghi_ready, 1)
                    nc.vector.tensor_tensor(glo[:, :, :], gw, ghi[:, :, :].bitcast(F32), ALU.subtract).then_inc(glo_ready, 1)
                    dve.wait_ge(pre_mm, 1)
                    nc.vector.tensor_copy(smallT[:, :], ps[:, MB, 0:36])
                    nc.vector.tensor_copy(vrev[:, :], ps[0:H, MB, 64:64 + SCORES]).then_inc(pre_evac, 1)
                    for t in range(TT):
                        last = nc.vector.tensor_copy(biasc[:, t].rearrange("p h c -> p c h"),
                                                     ps[:, OB, t * 240:(t + 1) * 240].rearrange("p (c h) -> p c h", h=H))
                    last.then_inc(pre_evac, 1)
                    chunk(2)
                    chunk(3)
                with dve.Fori(4 if s == 0 else 2, NCH - 1) as c:
                    chunk(c)
                hidden(f, u0, NCH - 2)
                for k in (31, 32):
                    lo_static(u0 + k)
                hidden(f, u0, NCH - 1, xhi, xlo, u0 + 31)
                for k in (33, 34):
                    lo_static(u0 + k)

            def attend(kind):
                n0, p0, N = STAGE0[kind], PAIR0[kind], STAGES[kind]
                per = 2 if kind == "nsa" else 1
                mask = cst[:, C_MASK:C_MASK + S]

                def logits(n):
                    b = n % PB
                    dve.wait_ge(scores_mm, n + 1)
                    if n >= PB:
                        dve.wait_ge(probT_mm, n - PB + 1)
                    for a in range(2):
                        for t, (c0, c1) in enumerate(((0, P), (P, SCORES))):
                            j0 = P if t == 0 else 0
                            add = bias[:, n, j0:S] if kind == "nsa" else mask[:, j0:S]
                            last = nc.vector.tensor_tensor_reduce(
                                out=prob[b][:, a, c0:c1], in0=ps[:, 2 * (n % 2) + a, c0:c1], in1=add, scale=-1.0, scalar=3e38,
                                op0=ALU.add, op1=ALU.min, accum_out=nmax[:, b, a, t:t + 1])
                    last.then_inc(logits_ready, 1)

                def factors(n):
                    b = n % PB
                    dve.wait_ge(exp_done, n + 1)
                    if kind == "nsa":
                        nc.vector.reciprocal(rsum[:, b], ssum[:, b]).then_inc(rsum_ready, 1)
                        dve.wait_ge(rsum_ready, n + 1)
                        g_ = gate[:, :, 16 + n:48:16].rearrange("p t a -> p a t")
                        nc.vector.tensor_tensor(fac[:, b], rsum[:, b], g_, ALU.mult).then_inc(fac_ready, 1)
                    else:
                        nc.vector.reciprocal(fac[:, b], ssum[:, b]).then_inc(fac_ready, 1)

                def probs_T(n):
                    b = n % 2
                    dve.wait_ge(probT_mm, n + 1)
                    if n >= 2:
                        dve.wait_ge(heads_mm, n - 1)
                    nc.vector.tensor_copy(probT[:, b], ps[:, GB:GB + 2, 0:SCORES]).then_inc(probT_ready, 1)

                def heads_lo(k):
                    dve.wait_ge(ohi_ready, p0 + k + 1)
                    nc.vector.tensor_tensor(xlo[:, k, :], ps[:, OB + k % 2, 0:S], xhi[:, k, :].bitcast(F32),
                                            ALU.subtract).then_inc(olo_ready, 1)
                for i in range(N + 4):
                    if 1 <= i < N + 1:
                        factors(n0 + i - 1)
                    if i < N:
                        logits(n0 + i)
                    if 2 <= i < N + 2:
                        probs_T(n0 + i - 2)
                    if i >= 4 and (i - 3) % per == 0:
                        heads_lo((i - 3) // per - 1)

            gain_input(0, 0)
            gain_input(0, 1)
            lo_static(0)
            split_x(0, 0)
            lo_static(1)
            split_x(0, 1)
            for s, kind in enumerate(KINDS):
                u0 = U0[s]
                if kind == "ffn":
                    ffn(s)
                else:
                    nproj = 10 if kind == "nsa" else 12

                    def gather(kv):
                        dve.wait_ge(pairs_in[kv], 64)
                        if kv:
                            dve.wait_ge(hid_mm, 1)
                        src = pairsv[:, :, :]
                        src = bass.AP(pairs[:, :].tensor, pairs[:, :].offset, [list(pairs[:, :].ap[0]), [2, 16], [S, G], [CS, NC]])
                        pe_ = smallT[:, 16 * kv:16 * kv + 16]
                        pe_ = bass.AP(pe_.tensor, pe_.offset, [list(pe_.ap[0]), [1, 16], [0, G], [0, NC]])
                        dst = flat[:, 0:960].rearrange("p (k g c) -> p k g c", k=16, g=G)
                        nc.vector.tensor_tensor(dst, src, pe_, ALU.add).then_inc(flat_ready, 1)
                    lo_static(u0 + 2)
                    for k in range(1, nproj):
                        lo_static(u0 + k + 2)
                        if kind == "nsa":
                            if k == 4:
                                dve.wait_ge(gate_exp, 1)
                                nc.vector.tensor_scalar(gate_e[:, :, :], gate_e[:, :, :], 1.0, None, ALU.add).then_inc(gate_step, 1)
                                dve.wait_ge(gate_step, 1)
                                nc.vector.reciprocal(gate[:, :, :], gate_e[:, :, :]).then_inc(gate_ready, 1)
                            if k == 5:
                                gather(0)
                            if k == 7:
                                dve.wait_ge(cmp_mm, 1)
                                nc.vector.tensor_copy(kcmp[:, :], ps[:, MB, 128:128 + G * NC]).then_inc(cmp_ready, 1)
                            if k == 7:
                                gather(1)
                            if k == 9:
                                dve.wait_ge(hid_ready, 2)
                                dve.wait_ge(hidR_zero, 1)
                                for m in range(2):
                                    src = hid[:, m, :]
                                    src = bass.AP(src.tensor, src.offset, [list(src.ap[0]), [NC, G], [0, 4], [1, NC]])
                                    last = nc.vector.tensor_copy(hidR[:, m, :, :, 0:NC], src)
                                last.then_inc(hidR_ready, 1)
                        elif k == 3:
                            dve.wait_ge(fT_mm, 1)
                            dve.wait_ge(bf_in, 32)
                            nc.vector.tensor_scalar(fT[:, 0, :], ps[0:32, MB, 0:S], bf[:, :], None, ALU.add).then_inc(f_step, 1)
                            dve.wait_ge(f_step, 1)
                            nc.vector.scalar_tensor_tensor(fT[:, 1, :], fT[:, 0, :], -1.0, fT[:, 0, :], ALU.mult, ALU.max).then_inc(f_step, 1)
                        elif k == 4:
                            dve.wait_ge(f_ln, 1)
                            nc.vector.scalar_tensor_tensor(fT[:, 1, :], fT[:, 0, :], 0.0, fT[:, 3, :], ALU.min, ALU.subtract).then_inc(f_step, 1)
                            dve.wait_ge(f_step, 3)
                            nc.vector.memset(rhsd[:, :], 0.0).then_inc(f_step, 1)
                            dve.wait_ge(f_step, 4)
                            nc.vector.tensor_tensor_scan(cum[:, :], rhsd[:, :], fT[:, 1, :], 0.0, ALU.add, ALU.add).then_inc(cum_ready, 1)
                            dve.wait_ge(cum_ready, 1)
                            nc.vector.tensor_scalar(rhsd[:, :], cum[:, :], cst[0:32, C_R:C_R + 1], cst[0:32, C_R + 1:C_R + 2],
                                                    ALU.mult, ALU.add).then_inc(f_step, 1)
                    if kind == "nsa":
                        dve.wait_ge(cmp_mm, 2)
                        nc.vector.tensor_copy(vcmp[:, :, :], ps[:, MB, 192:448].rearrange("p (g d) -> p g d", g=G)).then_inc(cmp_ready, 1)
                        dve.wait_ge(sc_mm, 1)
                        s3 = sc[:, :, :, :].rearrange("p t h c -> p (t h) c")
                        for r, bank in enumerate((OB, UB)):
                            last = nc.vector.tensor_tensor(sc[:, :, r:H:2, :], ps[:, bank, 0:240].rearrange("p (t h c) -> p t h c", t=TT, c=NC),
                                                           biasc[:, :, r:H:2, :], ALU.add)
                        last.then_inc(sc_step, 1)
                        dve.wait_ge(sc_step, 1)
                        nc.vector.tensor_reduce(cmx[:, :, :].rearrange("p t h -> p (t h)"), s3, AX.X, ALU.max).then_inc(sc_step, 1)
                        dve.wait_ge(sc_step, 2)
                        def spread(v):
                            return bass.AP(v[:, :, :].tensor, v[:, :, :].offset, [list(v[:, :, :].ap[0]), [1, TT * H], [0, NC]])
                        nc.vector.tensor_tensor(s3, s3, spread(cmx), ALU.subtract).then_inc(sc_logits, 1)
                        dve.wait_ge(sc_exp, 1)
                        nc.vector.tensor_reduce(csum[:, :, :].rearrange("p t h -> p (t h)"), s3, AX.X, ALU.add).then_inc(sc_step, 1)
                        dve.wait_ge(sc_step, 3)
                        nc.vector.reciprocal(cfac[:, :, :], csum[:, :, :]).then_inc(sc_step, 1)
                        dve.wait_ge(sc_step, 4)
                        for t in range(TT):
                            last = nc.vector.scalar_tensor_tensor(cfac[:, t, :], cfac[:, t, :], cst[:, C_VALID + t:C_VALID + t + 1],
                                                                  gate[:, t, 0:H], ALU.mult, ALU.mult)
                        last.then_inc(sc_step, 1)
                        dve.wait_ge(sc_step, 5)
                        dve.wait_ge(probc_zero, 1)
                        nc.vector.tensor_tensor(probc.rearrange("p t h c -> p (t h) c")[:, :, 0:NC], s3, spread(cfac), ALU.mult).then_inc(probc_ready, 1)
                        for t in range(TT):
                            dve.wait_ge(probcT_mm, t + 1)
                            nc.vector.tensor_copy(probcT[:, :, t * P:(t + 1) * P],
                                                  ps[:, MB - t, :].rearrange("p (g n) -> p g n", g=G)).then_inc(probcT_ready, 1)
                    attend(kind)
                    for k in range(4):
                        lo_static(u0 + nproj + k + 2)
                more = s + 1 < NSUB
                gain_output(s, 0)
                add_output(s, 0)
                if more:
                    gain_input(s + 1, 0)
                gain_output(s, 1)
                add_output(s, 1)
                if more:
                    split_x(s + 1, 0)
                    gain_input(s + 1, 1)
                    split_x(s + 1, 1)

        @block.tensor
        def _(pe):
            def mm(out_, l, r, start, stop):
                return nc.tensor.matmul(out_, l, r, start=start, stop=stop)

            def split_mm(out_, l, r, start, stop):
                (lh, ll), (rh, rl) = l, r
                mm(out_, lh, rh, start, False)
                mm(out_, lh, rl, False, False)
                return mm(out_, ll, rh, False, stop)

            def wcols(slot):
                return [w[:, slot, :].rearrange("p (k n) -> p k n", k=KT) for w in (whi, wlo)]

            def wrows(slot):
                return [w[:, slot, :].rearrange("p (k n) -> p k n", k=2) for w in (whi, wlo)]

            def features(u, slot, bank, between=None):
                pe.wait_ge(w_lo, u + 1)
                wh, wl = wcols(slot)
                for a in range(2):
                    if a == 1 and between:
                        between()
                    for k in range(KT):
                        last = split_mm(ps[:, bank, a * S:(a + 1) * S], (wh[:, k, a * P:(a + 1) * P], wl[:, k, a * P:(a + 1) * P]),
                                        (xhi[:, k, :], xlo[:, k, :]), k == 0, k == KT - 1)
                last.then_inc(unit_done, 1)

            def tokens(u, slot, bank, tiles=(0, 1)):
                pe.wait_ge(w_lo, u + 1)
                wh, wl = wcols(slot)
                for t in tiles:
                    for k in range(KT):
                        last = split_mm(ps[:, bank, t * UC:(t + 1) * UC], (xhi[:, k, t * P:(t + 1) * P], xlo[:, k, t * P:(t + 1) * P]),
                                        (wh[:, k, :], wl[:, k, :]), k == 0, k == KT - 1)
                if TT - 1 in tiles:
                    last.then_inc(unit_done, 1)

            def rows(u, slot, left, first, final):
                pe.wait_ge(w_lo, u + 1)
                wh, wl = wrows(slot)
                for k, t in [(k, t) for t in range(TT) for k in range(2)] if final else [(k, t) for k in range(2) for t in range(TT)]:
                    for b in range(2):
                        l = [v[:, t * P:(t + 1) * P] for v in left(k)]
                        last = split_mm(ps[:, YB + 2 * t + b, :], l, (wh[:, k, 512 * b:512 * b + 512], wl[:, k, 512 * b:512 * b + 512]),
                                        first and k == 0, final and k == 1)
                    if final and k == 1 and t == 0:
                        last.then_inc(y_ready, 1)
                last.then_inc(unit_done, 1)

            def transpose_input(s, t):
                pe.wait_ge(normed_ready, TT * s + t + 1)
                pe.wait_ge(diag_ready, TT * s + t + 1)
                for b in range(2):
                    for k in range(4):
                        last = mm(ps[:, GB + 2 * t + b, k * P:(k + 1) * P], normed[:, t, (4 * b + k) * P:(4 * b + k + 1) * P],
                                  diag[:, t, :], True, True)
                    last.then_inc(xT_ready, 1)

            def open_sublayer(s):
                u0 = U0[s]
                transpose_input(s, 0)
                pe.wait_ge(xlo_ready, 4 * s + 2)
                tokens(u0, u0 % RING, GB, (0,))
                transpose_input(s, 1)
                tokens(u0 + 1, (u0 + 1) % RING, UB, (0,))
                pe.wait_ge(xlo_ready, 4 * s + 4)
                tokens(u0, u0 % RING, GB, (1,))
                tokens(u0 + 1, (u0 + 1) % RING, UB, (1,))

            def setup():
                pe.wait_ge(small_in, 32)
                pe.wait_ge(cst_in, 16)
                nc.tensor.transpose(ps[:, MB, 0:36], small[:, :], cst[0:36, C_ID:C_ID + 36])
                pe.wait_ge(tab_in, 32)
                pe.wait_ge(oh_in, 16)
                for t in range(TT):
                    for c in range(NC):
                        m0 = t * P - (CS * c + CB - 1) + S
                        mm(ps[:, OB, t * 240 + c * H:t * 240 + (c + 1) * H], near[:, m0:m0 + P], tab[:, :], True, True)
                mm(ps[0:H, MB, 64:64 + SCORES], tab[:, :], back, True, True).then_inc(pre_mm, 1)

            def ffn(s):
                f, u0 = FFN_OF[s], U0[s]

                def first_T():
                    pe.wait_ge(prod_ready, NCH * f + 1)
                    for a in range(2):
                        for t in range(TT):
                            last = nc.tensor.transpose(ps[:, MB, a * S + t * P:a * S + (t + 1) * P],
                                                       prod_sb[:, t * UC + a * P:t * UC + (a + 1) * P], ident)
                    last.then_inc(prodT_mm, 1)

                def gate_(c, slot, first=False):
                    if not (isinstance(c, int) and c == 0):
                        pe.wait_ge(silu_ready, NCH * f + c)
                    features(G_(u0, c), slot, GB, first_T if first else None)

                def up_(c, slot):
                    if not (isinstance(c, int) and c == 0):
                        pe.wait_ge(prod_ready, NCH * f + c)
                    features(u0 + 1 + 3 * c, slot, UB)

                def down_(c, slot, first=False):
                    pe.wait_ge(hlo_ready, NCH * f + c + 1)
                    rows(u0 + 3 + 3 * c, slot, lambda k: (hhi[:, k, :], hlo[:, k, :]), first, False)

                def chunk(c, first=False):
                    gate_(c, (u0 + 2) % RING, first)
                    down_(c - 1, u0 % RING, first)
                    up_(c, (u0 + 1) % RING)
                chunk(1, True)
                if s == 0:
                    setup()
                    chunk(2)
                    chunk(3)
                    pe.wait_ge(skew_in, 16)
                    pe.wait_ge(pre_evac, 2)
                    for k in range(8):
                        if k >= 2:
                            pe.wait_ge(bias_ready, k - 1)
                        mm(ps[:, OB + k % 2, :], cst[:, C_J:C_J + P], skew[:, 2 * k:2 * k + 2, :], True, True).then_inc(bias_mm, 1)
                with pe.Fori(4 if s == 0 else 2, NCH - 1) as c:
                    chunk(c)
                gate_(NCH - 1, (u0 + 29) % RING)
                pe.wait_ge(prod_ready, NCH * f + NCH - 1)
                features(u0 + 30, (u0 + 30) % RING, UB)
                pe.wait_ge(hlo_ready, NCH * f + NCH - 1)
                rows(u0 + 31, (u0 + 31) % RING, lambda k: (hhi[:, k, :], hlo[:, k, :]), False, False)
                pe.wait_ge(hlo_ready, NCH * f + NCH)
                rows(u0 + 32, (u0 + 32) % RING, lambda k: (xhi[:, k, :], xlo[:, k, :]), False, True)

            def gates(n, c0, w):
                pe.wait_ge(glo_ready, 1)
                for t in range(TT):
                    for k in range(KT):
                        last = split_mm(ps[:, OB, t * w:(t + 1) * w], (xhi[:, k, t * P:(t + 1) * P], xlo[:, k, t * P:(t + 1) * P]),
                                        (ghi[:, k, c0:c0 + w], glo[:, k, c0:c0 + w]), k == 0, k == KT - 1)
                last.then_inc(gates_mm, 1)

            def compress_hidden(kv):
                pe.wait_ge(flat_ready, kv + 1)
                pe.wait_ge(w1_in[kv], 16)
                if kv:
                    pe.wait_ge(hid_ready, 1)
                    pe.wait_ge(cmp_ready, 1)
                for m in range(2):
                    for k in range(16):
                        last = mm(ps[:, MB, m * 64:m * 64 + G * NC], w1[:, k, m * P:(m + 1) * P], flatv[:, k, :], k == 0, k == 15)
                last.then_inc(hid_mm, 1)

            def compress_out(kv):
                if kv == 0:
                    pe.wait_ge(w2_in, 48)
                    pe.wait_ge(hid_ready, 1)
                    for m in range(2):
                        last = mm(ps[:, MB, 128:128 + G * NC], w2k[:, m, :, :].rearrange("p r d -> p (r d)"), hid[:, m, :], m == 0, m == 1)
                else:
                    pe.wait_ge(hidR_ready, 1)
                    for g in range(G):
                        for m in range(2):
                            last = mm(ps[:, MB, 192 + g * DH:192 + (g + 1) * DH], hidR[:, m, g, :, :].rearrange("p r c -> p (r c)"),
                                      w2v[:, m, :], m == 0, m == 1)
                last.then_inc(cmp_mm, 1)

            def attend(kind, between=None):
                n0, p0, N = STAGE0[kind], PAIR0[kind], STAGES[kind]
                per = 2 if kind == "nsa" else 1

                def side(h):
                    return slice(64 * (h % 2), 64 * (h % 2) + 64)

                def keys(n, a):
                    if kind == "nsa":
                        h, g = n, n // G
                        k_ = kN if h % 2 == g % 2 else kX
                        return h, k_[side(h), a, g // 2, :]
                    h = 2 * (n - n0) + a
                    return h, kF[side(h), h // 2, :]

                def values(n, a, t):
                    if kind == "nsa":
                        return vN[:, a, t, (n // G) * DH:(n // G + 1) * DH]
                    h = 2 * (n - n0) + a
                    return vF[:, t, h * DH:(h + 1) * DH]

                def scores(n):
                    b = n % 2
                    if n >= 2:
                        pe.wait_ge(logits_ready, n - 1)
                    for a in range(2):
                        h, k_ = keys(n, a)
                        for t, (c0, c1) in enumerate(((0, P), (P, SCORES))):
                            o_ = ps[:, 2 * b + a, c0:c1]
                            last = mm(o_, qT[side(h), h // 2, t * P:(t + 1) * P], k_[:, 0:c1 - c0], True, kind == "nsa")
                            if kind == "fox":
                                last = mm(o_, bias[0:32, h, t * P:(t + 1) * P], rhsd[:, 0:c1 - c0], False, True)
                    last.then_inc(scores_mm, 1)

                def probs_T(n):
                    b = n % PB
                    pe.wait_ge(prob_ready, n + 1)
                    if n >= 1:
                        pe.wait_ge(probT_ready, n)
                    for a in range(2):
                        for k in range(3):
                            last = nc.tensor.transpose(ps[:, GB + a, k * P:(k + 1) * P], prob[b][:, a, k * P:(k + 1) * P], ident)
                    last.then_inc(probT_mm, 1)

                def heads(n):
                    b = n % 2
                    pe.wait_ge(probT_ready, n + 1)
                    pair = (n - n0) // per
                    if pair >= 2:
                        pe.wait_ge(olo_ready, p0 + pair - 1)
                    bank = OB + pair % 2
                    for a in range(2):
                        half_ = side(n) if kind == "nsa" else side(a)
                        start = kind == "fox" or a == 0
                        if kind == "nsa" and a == 0:
                            r = 32 * (n % G)
                            mm(ps[half_, bank, 0:S], vcmp[r:r + 32, n // G, :], probcT[r:r + 32, n // G, :], True, False)
                            start = False
                        mm(ps[half_, bank, 0:S], values(n, a, 0), probT[:, b, a, 0:S], start, False)
                        last = mm(ps[half_, bank, P:S], values(n, a, 1), probT[:, b, a, S:SCORES], False, kind == "fox" or a == 1)
                    last.then_inc(heads_mm, 1)
                for i in range(N + 3):
                    if i < N:
                        scores(n0 + i)
                    if between and i == 1:
                        between()
                    if 2 <= i < N + 2:
                        probs_T(n0 + i - 2)
                    if i >= 3:
                        heads(n0 + i - 3)

            for s, kind in enumerate(KINDS):
                u0 = U0[s]
                open_sublayer(s)
                if kind == "ffn":
                    ffn(s)
                    continue
                pr0 = PROJ0[kind]
                nproj = 10 if kind == "nsa" else 12
                for k in range(nproj):
                    if k >= 2:
                        pe.wait_ge(proj_ready, pr0 + k - 1)
                        by_token = kind == "fox" and k < 4
                        (tokens if by_token else features)(u0 + k, (u0 + k) % RING, GB + k % 2)
                    if kind == "nsa" and k == 2:
                        gates(0, 0, 48)
                    if kind == "nsa" and k in (5, 8):
                        compress_hidden((k - 5) // 3)
                    if kind == "nsa" and k in (6, 9):
                        compress_out((k - 6) // 3)
                    if kind == "fox" and k == 1:
                        gates(1, 48, 16)
                    if kind == "fox" and k == 2:
                        pe.wait_ge(fz_ready, 1)
                        for t in range(TT):
                            last = nc.tensor.transpose(ps[0:32, MB, t * P:(t + 1) * P], fz[:, t, :], ident)
                        last.then_inc(fT_mm, 1)
                pe.wait_ge(proj_ready, pr0 + nproj)
                if kind == "nsa":
                    pe.wait_ge(gate_exp, 1)
                    for t in range(TT):
                        for h in range(H):
                            sd = slice(64 * (h % 2), 64 * (h % 2) + 64)
                            g = h // G
                            c0 = (t * H // 2 + h // 2) * NC
                            last = mm(ps[:, (OB, UB)[h % 2], c0:c0 + NC], qT[sd, h // 2, t * P:(t + 1) * P],
                                      kcmp[sd, g * NC:(g + 1) * NC], True, True)
                    last.then_inc(sc_mm, 1)
                    pe.wait_ge(kx_in, 64)

                    def compressed_T():
                        pe.wait_ge(probc_ready, 1)
                        pe.wait_ge(cmp_ready, 2)
                        for t in range(TT):
                            for g in range(G):
                                last = nc.tensor.transpose(ps[:, MB - t, g * P:(g + 1) * P],
                                                           probc[:, t, G * g:G * g + G, :].rearrange("p h c -> p (h c)"), ident)
                            last.then_inc(probcT_mm, 1)
                        pe.wait_ge(probcT_ready, 2)
                    attend(kind, compressed_T)
                else:
                    pe.wait_ge(decay_ready, 1)
                    pe.wait_ge(f_step, 5)
                    attend(kind)
                for k in range(4):
                    pe.wait_ge(olo_ready, PAIR0[kind] + 2 * k + 2)
                    u = u0 + nproj + k
                    rows(u, u % RING, lambda j: (xhi[:, 2 * k + j, :], xlo[:, 2 * k + j, :]), k == 0, k == 3)


_INS = ["x", "norm_g", "ffn_w_gate", "ffn_w_up", "ffn_w_down", "rel_bias", "nsa_w_in", "nsa_cmp_pe",
        "nsa_cmp_w1", "nsa_cmp_b1", "nsa_cmp_w2", "nsa_w_out", "fox_w_in", "fox_b_f", "fox_w_out"]


def kernel(**inputs):
    import concourse.bacc as _bacc
    from concourse.bass_utils import run_bass_kernel_spmd as _run

    nc = _bacc.Bacc("TRN2", target_bir_lowering=False, num_devices=1)
    arrays, args = {}, []
    consts, onehots = tables()
    for name, a in [(n, inputs[n]) for n in _INS] + [("consts", consts), ("onehots", onehots)]:
        a = np.ascontiguousarray(a)
        arrays[f"in_{name}"] = a
        args.append(nc.dram_tensor(f"in_{name}", a.shape, mybir.dt.from_np(a.dtype), kind="ExternalInput").ap())
    args.append(nc.dram_tensor("out_0", (1, S, D), F32, kind="ExternalOutput").ap())
    args.append(nc.dram_tensor("scratch", (H, SCORES), F32, kind="Internal").ap())
    trunk(nc, *args)
    r = _run(nc, [arrays], core_ids=[0])
    return r.results[0]["out_0"]
```

```python
from contextlib import ExitStack

import numpy as np

import concourse.bass as bass
from concourse import mybir

F32 = mybir.dt.float32
F32R = mybir.dt.float32r
ALU = mybir.AluOpType
ACT = mybir.ActivationFunctionType
AX = mybir.AxisListType

P = 128
D = 1024
S = 256
KT = D // P
TT = S // P
FF = 2816
UC = 256
NCH = FF // UC
H = 16
DH = 64
G = 4
CB, CS = 32, 16
NC = (S - CB) // CS + 1
CP = 32
HID = 256
NB = 32
NEG = -1e30
EPS = 1e-6
RING = 3
IDLE_START, IDLE_BOUNDARY = 8, 7
LAG = 3
PB = LAG + 1
SCORES = S + P

KINDS = ["ffn", "nsa", "ffn", "ffn", "fox", "ffn"]
UNITS = {"ffn": 3 * NCH, "nsa": 14, "fox": 16}
U0 = [sum(UNITS[k] for k in KINDS[:s]) for s in range(len(KINDS))]
NUNITS = sum(UNITS[k] for k in KINDS)
NSUB = len(KINDS)
FFN_OF = {0: 0, 2: 1, 3: 2, 5: 3}
WHICH = [(0, 0), None, (0, 1), (1, 0), None, (1, 1)]
NORM = [(0, 0), (0, 2), (0, 4), (1, 0), (1, 2), (1, 4)]

C_ID, C_J, C_MASK, C_VALID, C_A1, C_A2, C_R, C_NEG, C_SEL = 0, 128, 256, 512, 514, 530, 546, 548, 564
C_END = 564 + P
GWC = 48 + 2 * H


def t5_bucket(rel):
    n = np.maximum(rel, 0)
    nf = np.maximum(n, 1).astype(np.float32)
    large = 16 + (np.log(nf / np.float32(16)) / np.float32(np.log(8.0)) * np.float32(16)).astype(np.int32)
    return np.where(n < 16, n, np.minimum(large, NB - 1))


def tables():
    c = np.zeros((P, C_END), np.float32)
    c[:, C_ID:C_ID + P] = np.eye(P)
    c[:, C_J:C_J + P] = np.eye(P)[::-1]
    p, j = np.arange(P)[:, None], np.arange(S)[None, :]
    c[:, C_MASK:C_MASK + S] = np.where(P + p - j >= 0, 0.0, NEG)
    for t in range(TT):
        c[:, C_VALID + t] = np.arange(P) + t * P >= CB - 1
    for r in (0, 64):
        for h in range(H):
            c[r + h, C_A1 + h] = 1.0
            c[r + H + h, C_A2 + h] = 1.0
        c[r + H:r + 2 * H, C_R] = -1.0
        c[r:r + H, C_R + 1] = 1.0
        c[0:2 * H, C_SEL + r:C_SEL + r + 2 * H] = np.eye(2 * H)
    c[NB, C_NEG:C_NEG + H] = NEG

    def onehot(rel):
        o = np.zeros((NB + 1, len(rel)), np.float32)
        o[np.where(rel < 0, NB, t5_bucket(rel)), np.arange(len(rel))] = 1.0
        return o

    return c, onehot(S - 1 - np.arange(SCORES))


def trunk(nc, x, norm_g, w_gate, w_up, w_down, rel_bias, nsa_in, cmp_pe, cmp_w1, cmp_b1, cmp_w2,
          nsa_out, fox_in, fox_bf, fox_out, consts, onehots, out, scratch):
    with ExitStack() as ctx:
        def sb(name, shape, dt=F32):
            return ctx.enter_context(nc.sbuf_tensor(name, shape, dt))

        def sem(name):
            return ctx.enter_context(nc.semaphore(name))

        raw = sb("raw", [P, RING, 2048])
        whi = sb("whi", [P, RING, 2048], F32R)
        wlo = sb("wlo", [P, RING, 2048], F32R)
        res = sb("res", [P, TT, D])
        xhi = sb("xhi", [P, KT, S], F32R)
        xlo = sb("xlo", [P, KT, S], F32R)
        hhi = sb("hhi", [P, 2, S], F32R)
        hlo = sb("hlo", [P, 2, S], F32R)
        work = sb("work", [P, 4 * SCORES])
        silu_sb = work[:, 0:512]
        prod_sb = work[:, 512:1024]
        g_pre = sb("g_pre", [P, D])
        g_post = sb("g_post", [P, D])
        normed = sb("normed", [P, TT, D])
        prob = [v.rearrange("p (a n) -> p a n", a=2) for v in
                (work[:, 0:2 * SCORES], work[:, 2 * SCORES:4 * SCORES], normed[:, 0, 0:2 * SCORES], normed[:, 1, 0:2 * SCORES])]
        big = sb("big", [P, 4096])
        skew = big[:, :].rearrange("p (h n) -> p h n", h=H)
        w1 = big[:, :].rearrange("p (k n) -> p k n", k=16)
        kF = big[:, 0:2048].rearrange("p (k n) -> p k n", k=KT)
        vF = big[:, 2048:4096].rearrange("p (t n) -> p t n", t=TT)
        bias = sb("bias", [P, H, S])
        kcv = work[:, 0:1024].rearrange("p (r g t) -> p r g t", r=2, g=2)
        kN = sb("kN", [P, 2, 2, S])
        kX = sb("kX", [P, 2, 2, S])
        vN = sb("vN", [P, 2, TT, S])
        qT = sb("qT", [P, KT, S])
        pairs = sb("pairs", [P, 1024])
        pairsv = pairs[:, :].rearrange("p (g t) -> p g t", g=G)
        probc = pairs[:, :].rearrange("p (t h c) -> p t h c", t=TT, h=H)
        back = pairs[0:NB + 1, 0:SCORES]
        flat = sb("flat", [P, 1024])
        flatv = flat[:, 0:16 * G * NC].rearrange("p (k n) -> p k n", k=16)
        gw = flat[:, 0:KT * GWC].rearrange("p (k n) -> p k n", k=KT)
        probcT = flat[:, :].rearrange("p (g t) -> p g t", g=G)
        ghi = sb("ghi", [P, KT, GWC], F32R)
        glo = sb("glo", [P, KT, GWC], F32R)
        probT_buf = sb("probT_buf", [P, 4 * SCORES])
        probT = probT_buf[:, :].rearrange("p (b a n) -> p b a n", b=2, a=2)
        hidR = probT_buf[:, 0:1024].rearrange("p (m g r c) -> p m g r c", m=2, g=G, r=4)
        sc = sb("sc", [P, TT, H, NC])
        hid = sb("hid", [P, 2, G * NC])
        kcmp = sb("kcmp", [P, G, 2, NC])
        vcmp = sb("vcmp", [P, G, DH])
        w2k = sb("w2k", [P, 2, 2, DH])
        w2v = sb("w2v", [P, 2, DH])
        cst = sb("cst", [P, C_END])
        tab = sb("tab", [NB + 1, H])
        small = sb("small", [36, P])
        smallT = sb("smallT", [P, 36])
        vrev = sb("vrev", [H, SCORES])
        gate_e = work[0:48, 1024:1024 + S]
        gateT = work[0:48, 1024 + S:1024 + 2 * S]
        gate = sb("gate", [P, TT, 48])
        fT = pairs[0:32, :].rearrange("p (k t) -> p k t", k=4)
        cum = flat[0:32, 0:S]
        zeros = flat[0:32, S:2 * S]
        cum_wide = flat[:, 2 * S:3 * S]
        qF = [qT, bias[:, 0:KT, :]]
        kFs = [kF, bias[:, KT:2 * KT, :]]
        bf = sb("bf", [32, 1])
        ss = sb("ss", [P, 4 * NSUB])
        ss_half = sb("ss_half", [P, TT * NSUB])
        ms_half = sb("ms_half", [P, TT * NSUB])
        ms = sb("ms", [P, 4 * NSUB])
        rstd = sb("rstd", [P, 4 * NSUB])
        half = sb("half", [P, 1])
        nmax = sb("nmax", [P, PB, 2, TT])
        ssum = sb("ssum", [P, PB, 2, TT])
        rsum = sb("rsum", [P, PB, 2, TT])
        fac = sb("fac", [P, PB, 2, TT])
        cmx = sb("cmx", [P, TT, H])
        csum = sb("csum", [P, TT, H])
        cfac = sb("cfac", [P, TT, H])
        ps = ctx.enter_context(nc.psum_tensor("ps", [P, 8, 512], F32))
        ident = cst[:, C_ID:C_ID + P]
        YB, GB, UB, OB, MB = 0, 4, 5, 6, 7

        raw_in = [sem(f"raw_in{i}") for i in range(RING)]
        w_hi, w_lo, unit_done = sem("w_hi"), sem("w_lo"), sem("unit_done")
        res_in = [sem("res0_in"), sem("res1_in")]
        ident_in, first_hi = sem("ident_in"), sem("first_hi")
        second_hi = sem("second_hi")
        cst_in, gw_in, small_in = sem("cst_in"), sem("gw_in"), sem("small_in")
        tab_in, oh_in, w2_in, bf_in = sem("tab_in"), sem("oh_in"), sem("w2_in"), sem("bf_in")
        gpre_in, gpost_in = sem("gpre_in"), sem("gpost_in")
        half_set = sem("half_set")
        sumsq, mean_ready, rstd_ready = sem("sumsq"), sem("mean_ready"), sem("rstd_ready")
        y_ready, yg_ready, res_ready, normed_ready = (
            sem("y_ready"), sem("yg_ready"), sem("res_ready"), sem("normed_ready"))
        res_half, half_sumsq, half_mean = sem("res_half"), sem("half_sumsq"), sem("half_mean")
        xT_ready, xhi_ready, xlo_ready = sem("xT_ready"), sem("xhi_ready"), sem("xlo_ready")
        silu_ready, prod_ready, hhi_ready, hlo_ready = sem("silu_ready"), sem("prod_ready"), sem("hhi_ready"), sem("hlo_ready")
        prodT_mm = sem("prodT_mm")
        ghi_ready, glo_ready = sem("ghi_ready"), sem("glo_ready")
        pre_mm, pre_evac = sem("pre_mm"), sem("pre_evac")
        vrev_out, skew_in = sem("vrev_out"), sem("skew_in")
        bias_mm, bias_ready = sem("bias_mm"), sem("bias_ready")
        proj_ready = sem("proj_ready")
        w1_in = [sem("w1k_in"), sem("w1v_in")]
        pairs_in = [sem("pairsk_in"), sem("pairsv_in")]
        kx_in = sem("kx_in")
        gates_mm, gate_exp, gate_step, gate_ready, gateT_mm = sem("gates_mm"), sem("gate_exp"), sem("gate_step"), sem("gate_ready"), sem("gateT_mm")
        kcmp_zero = sem("kcmp_zero")
        flat_ready, hid_mm, hid_ready, hidR_zero, hidR_ready = sem("flat_ready"), sem("hid_mm"), sem("hid_ready"), sem("hidR_zero"), sem("hidR_ready")
        cmp_mm, cmp_ready = sem("cmp_mm"), sem("cmp_ready")
        sc_mm, sc_step, sc_logits, sc_exp = sem("sc_mm"), sem("sc_step"), sem("sc_logits"), sem("sc_exp")
        probc_zero, probc_ready, probcT_mm, probcT_ready = sem("probc_zero"), sem("probc_ready"), sem("probcT_mm"), sem("probcT_ready")
        scores_mm, logits_ready, exp_done = sem("scores_mm"), sem("logits_ready"), sem("exp_done")
        rsum_ready, fac_ready, prob_ready = sem("rsum_ready"), sem("fac_ready"), sem("prob_ready")
        probT_mm, probT_ready, heads_mm = sem("probT_mm"), sem("probT_ready"), sem("heads_mm")
        ohi_ready, olo_ready = sem("ohi_ready"), sem("olo_ready")
        f_step, f_exp, f_ln, cum_ready, cum_mm, wide_ready, decay_ready = (
            sem("f_step"), sem("f_exp"), sem("f_ln"), sem("cum_ready"), sem("cum_mm"), sem("wide_ready"), sem("decay_ready"))
        stored = sem("stored")

        STAGE0 = {"nsa": 0, "fox": H}
        PAIR0 = {"nsa": 0, "fox": 8}
        PROJ0 = {"nsa": 0, "fox": 10}
        STAGES = {"nsa": H, "fox": H // 2}

        def norm_index(s, post, t):
            if s == 0 and not post:
                return t
            if s == NSUB - 1 and post:
                return 4 * s + 2 + t
            return (4 * s + 2 + 2 * t) if post else (4 * s - 1 + 2 * t)

        def gate_unit(u0, c):
            return u0 if isinstance(c, int) and c == 0 else u0 - 1 + 3 * c

        def wait_output(engine, s, t):
            if t == 0:
                engine.wait_ge(y_ready, s + 1)
            else:
                engine.wait_ge(unit_done, U0[s] + UNITS[KINDS[s]])

        block = ctx.enter_context(nc.Block())

        @block.sync
        def _(sp):
            def load(u, slot, parts, src):
                if not (isinstance(u, int) and u < RING):
                    sp.wait_ge(w_lo, u - RING + 1)
                dst = raw[:, slot, :].rearrange("p (a n) -> p a n", a=parts)
                sp.dma_start(dst, src).then_inc(raw_in[slot], 16)

            def load_cols(u, slot, w, c0):
                load(u, slot, KT, w[:, bass.ds(c0, UC)].rearrange("(k p) n -> p k n", p=P))

            def load_rows(u, slot, w, r0):
                load(u, slot, 2, w[bass.ds(r0, UC), :].rearrange("(k p) n -> p k n", p=P))

            def load_small():
                sp.dma_start(cst[:, P:C_END], consts[:, P:C_END]).then_inc(cst_in, 16)
                sp.dma_start(pairs[0:NB + 1, 0:SCORES], onehots).then_inc(oh_in, 16)
                sp.dma_start(tab[0:NB, :], rel_bias).then_inc(tab_in, 16)
                sp.dma_start(tab[NB:NB + 1, :], consts[NB:NB + 1, C_NEG:C_NEG + H]).then_inc(tab_in, 16)
                sp.dma_start(small[0:32, :], cmp_pe[0].rearrange("v (k q) d -> (v k) (q d)", q=2)).then_inc(small_in, 16)
                sp.dma_start(small[32:36, :], cmp_b1[0].rearrange("v (m q) -> (v m) q", q=P)).then_inc(small_in, 16)
                sp.dma_start(gw[:, :, 0:48], nsa_in[0][:, 2560:2608].rearrange("(k p) n -> p k n", p=P)).then_inc(gw_in, 16)
                for r in range(2):
                    sp.dma_start(gw[:, :, 48 + H * r:48 + H * r + H], fox_in[0][:, 3072:3088].rearrange("(k p) n -> p k n", p=P)).then_inc(gw_in, 16)
                    sp.dma_start(bf[H * r:H * r + H, :], fox_bf[0].rearrange("(h a) -> h a", a=1)).then_inc(bf_in, 16)
                for r in range(2):
                    sp.dma_start(w2k[:, :, r, :], cmp_w2[0, 0].rearrange("(m p) n -> p m n", p=P)).then_inc(w2_in, 16)
                sp.dma_start(w2v[:, :, :], cmp_w2[0, 1].rearrange("(m p) n -> p m n", p=P)).then_inc(w2_in, 16)

            def load_x(t):
                sp.dma_start(res[:, t, :], x[0, t * P:(t + 1) * P, :]).then_inc(res_in[t], 16)

            load_x(0)
            for s, kind in enumerate(KINDS):
                u0 = U0[s]
                if kind == "ffn":
                    i, m = WHICH[s]
                    load_cols(u0, u0 % RING, w_gate[i, m], 0)
                    if s == 0:
                        load_x(1)
                    load_cols(u0 + 1, (u0 + 1) % RING, w_up[i, m], 0)
                    if s == 0:
                        load_small()
                    with sp.Fori(1, NCH - 1) as c:
                        load_cols(u0 - 1 + 3 * c, (u0 + 2) % RING, w_gate[i, m], c * UC)
                        load_rows(u0 + 3 * c, u0 % RING, w_down[i, m], c * UC - UC)
                        load_cols(u0 + 1 + 3 * c, (u0 + 1) % RING, w_up[i, m], c * UC)
                    load_cols(u0 + 29, (u0 + 29) % RING, w_gate[i, m], (NCH - 1) * UC)
                    load_cols(u0 + 30, (u0 + 30) % RING, w_up[i, m], (NCH - 1) * UC)
                    load_rows(u0 + 31, (u0 + 31) % RING, w_down[i, m], (NCH - 2) * UC)
                    load_rows(u0 + 32, (u0 + 32) % RING, w_down[i, m], (NCH - 1) * UC)
                else:
                    w, wo = (nsa_in[0], nsa_out[0]) if kind == "nsa" else (fox_in[0], fox_out[0])
                    cols = [1792, 2304, 1024, 1280, 1536, 2048, 0, 256, 512, 768] if kind == "nsa" else [UC * k for k in (8, 9, 10, 11, 0, 1, 2, 3, 4, 5, 6, 7)]
                    for k, c0 in enumerate(cols):
                        load_cols(u0 + k, (u0 + k) % RING, w, c0)
                    for k in range(4):
                        u = u0 + len(cols) + k
                        load_rows(u, u % RING, wo, k * UC)
            for t in range(TT):
                for cols, signal in ((slice(0, 512), res_half), (slice(512, 1024), res_ready)):
                    sp.wait_ge(signal, TT * (NSUB - 1) + t + 1)
                    sp.dma_start(out[0, t * P:(t + 1) * P, cols], res[:, t, cols]).then_inc(stored, 16)
            sp.wait_ge(stored, 16 * 2 * TT)

        @block.gpsimd
        def _(pool):
            def rstd_of(s, post, t):
                scale = 4.0 if post and KINDS[s] == "ffn" else 1.0
                i = norm_index(s, post, t)
                eps = scale * EPS
                if not post and s > 0:
                    j = TT * (s - 1) + t
                    pool.wait_ge(half_sumsq, j + 1)
                    nc.gpsimd.tensor_scalar(ms_half[:, j:j + 1], ss_half[:, j:j + 1], scale / D, eps, ALU.mult, ALU.add).then_inc(half_mean, 1)
                    pool.wait_ge(half_mean, j + 1)
                    eps = ms_half[:, j:j + 1]
                pool.wait_ge(sumsq, i + 1)
                nc.gpsimd.tensor_scalar(ms[:, i:i + 1], ss[:, i:i + 1], scale / D, eps, ALU.mult, ALU.add).then_inc(mean_ready, 1)
                pool.wait_ge(mean_ready, i + 1)
                nc.gpsimd.tensor_tensor(rstd[:, i:i + 1], ms[:, i:i + 1], half[:, :], ALU.pow).then_inc(rstd_ready, 1)

            def between_sublayers(s):
                for t in range(TT):
                    rstd_of(s, 1, t)
                    if s + 1 < NSUB:
                        rstd_of(s + 1, 0, t)

            def load_gain(s, post):
                i, n = NORM[s]
                dst, signal = (g_post, gpost_in) if post else (g_pre, gpre_in)
                if s > 0:
                    pool.wait_ge(yg_ready if post else normed_ready, TT * s if post else 2 * TT * s)
                pool.dma_start(dst[:, :], bass.AP(norm_g.tensor, (i * 6 + n + post) * D, [[0, P], [1, D]])).then_inc(signal, 16)

            def scale_probs(n):
                b = n % PB
                pool.wait_ge(fac_ready, n + 1)
                for a in range(2):
                    for t, (c0, c1) in enumerate(((0, P), (P, SCORES))):
                        p_ = prob[b][:, a, c0:c1]
                        last = nc.gpsimd.tensor_scalar(p_, p_, fac[:, b, a, t:t + 1], 1.0, ALU.mult, ALU.mult)
                last.then_inc(prob_ready, 1)

            nc.gpsimd.memset(half[:, :], -0.5).then_inc(half_set, 1)
            load_gain(0, 0)
            pool.wait_ge(half_set, 1)
            for t in range(TT):
                rstd_of(0, 0, t)
            pool.wait_ge(pre_evac, 1)
            pool.dma_start(scratch, vrev[:, :]).then_inc(vrev_out, 16)
            pool.wait_ge(vrev_out, 16)
            pool.dma_start(skew, bass.AP(scratch.tensor, 0, [[1, P], [SCORES, H], [1, S]])).then_inc(skew_in, 16)
            load_gain(0, 1)
            load_gain(1, 0)
            pool.wait_ge(bias_mm, 8)
            pool.dma_start(w1, cmp_w1[0, 0].rearrange("(k p) n -> p k n", p=P)).then_inc(w1_in[0], 16)
            between_sublayers(0)

            load_gain(1, 1)
            load_gain(2, 0)
            def pair_tokens(kv):
                pool.wait_ge(proj_ready, kv + 3)
                if kv:
                    pool.wait_ge(flat_ready, 1)
                for a in range(2):
                    src = kcv[64 * a:64 * a + 64, kv, :, :]
                    pool.dma_start(pairsv[0:64, a:G:2, :], src).then_inc(pairs_in[kv], 16)
                    pool.dma_start(pairsv[64:128, a:G:2, 0:S - 1], src[:, :, 1:S]).then_inc(pairs_in[kv], 16)

            nc.gpsimd.memset(kcmp[:, :, :, :], 0.0).then_inc(kcmp_zero, 1)
            pair_tokens(0)
            for r in range(2):
                pool.wait_ge(proj_ready, 5 + r)
                for a in range(2):
                    pool.dma_start(kX[64 * (1 - a):64 * (1 - a) + 64, r, :, :], kN[64 * a:64 * a + 64, r, :, :]).then_inc(kx_in, 16)
            pair_tokens(1)
            pool.wait_ge(hid_mm, 1)
            pool.dma_start(w1, cmp_w1[0, 1].rearrange("(k p) n -> p k n", p=P)).then_inc(w1_in[1], 16)
            nc.gpsimd.memset(probT_buf[:, 0:1024], 0.0).then_inc(hidR_zero, 1)
            pool.wait_ge(flat_ready, 2)
            nc.gpsimd.memset(pairs[:, :], 0.0).then_inc(probc_zero, 1)
            for n in range(H):
                scale_probs(n)
            between_sublayers(1)
            for s in range(2, NSUB):
                load_gain(s, 1)
                if s + 1 < NSUB:
                    load_gain(s + 1, 0)
                if KINDS[s] == "fox":
                    pool.wait_ge(wide_ready, 1)
                    for h in range(H):
                        o_ = slice(64 * (1 - h % 2), 64 * (1 - h % 2) + 64)
                        last = nc.gpsimd.tensor_scalar(qF[h % 2][o_, h // 2, :], cum_wide[o_, :], cst[o_, C_A1 + h:C_A1 + h + 1],
                                                       cst[o_, C_A2 + h:C_A2 + h + 1], ALU.mult, ALU.add)
                    last.then_inc(decay_ready, 1)
                    for n in range(H, H + H // 2):
                        scale_probs(n)
                between_sublayers(s)

        @block.scalar
        def _(act):
            def hi(u, slot, uses):
                act.wait_ge(raw_in[slot], 16 * uses)
                if not (isinstance(u, int) and u < RING):
                    act.wait_ge(unit_done, u - RING + 1)
                nc.scalar.activation(whi[:, slot, :], raw[:, slot, :], ACT.Copy).then_inc(w_hi, 1)

            def hi_static(u):
                if u < NUNITS:
                    hi(u, u % RING, u // RING + 1)

            def square(s, post, t):
                i = norm_index(s, post, t)
                if post:
                    src = ps[:, YB + 2 * t:YB + 2 * t + 2, :]
                    wait_output(act, s, t)
                elif s == 0:
                    src = res[:, t, :].rearrange("p (a n) -> p a n", a=2)
                    act.wait_ge(res_in[t], 16)
                if i >= 1:
                    act.wait_ge(sumsq, i)
                if not post and s > 0:
                    j = TT * (s - 1) + t
                    act.wait_ge(res_half, j + 1)
                    nc.scalar.activation(ps[:, OB, :], res[:, t, 0:512], ACT.Square, accum_out=ss_half[:, j:j + 1]).then_inc(half_sumsq, 1)
                    act.wait_ge(res_ready, j + 1)
                    nc.scalar.activation(ps[:, MB, :], res[:, t, 512:1024], ACT.Square, accum_out=ss[:, i:i + 1]).then_inc(sumsq, 1)
                    return
                nc.scalar.activation(ps[:, OB:OB + 2, :], src, ACT.Square, accum_out=ss[:, i:i + 1]).then_inc(sumsq, 1)

            def split_x(s, t):
                for b in range(2):
                    i = 4 * s + 2 * t + b
                    act.wait_ge(xT_ready, i + 1)
                    src = ps[:, GB + 2 * t + b, :].rearrange("p (k n) -> p k n", k=4)
                    nc.scalar.activation(xhi[:, 4 * b:4 * b + 4, t * P:(t + 1) * P], src, ACT.Copy).then_inc(xhi_ready, 1)

            def silu(f, u0, c, first=False):
                act.wait_ge(unit_done, gate_unit(u0, c) + 1)
                if not (isinstance(c, int) and c == 0 and f == 0):
                    act.wait_ge(prod_ready, NCH * f + c)
                nc.scalar.activation(silu_sb, ps[:, GB, :], ACT.Silu).then_inc(silu_ready, 1)

            def hidden_hi(f, c, dst=hhi):
                if isinstance(c, int) and c == 0:
                    act.wait_ge(prodT_mm, f + 1)
                    src = ps[:, MB, :]
                else:
                    act.wait_ge(prod_ready, NCH * f + c + 1)
                    src = prod_sb
                nc.scalar.activation(dst[:, 0:2, :], src.rearrange("p (a n) -> p a n", a=2), ACT.Copy).then_inc(hhi_ready, 1)

            def ffn(s):
                f, u0 = FFN_OF[s], U0[s]

                def chunk(c):
                    r = u0 // RING + c
                    dyn = not isinstance(c, int)

                    def split(k):
                        if dyn or u0 + 3 * c + k < NUNITS:
                            hi(u0 + k + 3 * c, (u0 + k) % RING, (u0 + k) // RING + 1 + c)
                    hidden_hi(f, c - 1)
                    split(1)
                    silu(f, u0, c)
                    split(2)
                    split(3)
                hi_static(u0 + 2)
                silu(f, u0, 0)
                hi_static(u0 + 3)
                chunk(1)
                if s == 0:
                    act.wait_ge(gw_in, 16 * 3)
                    nc.scalar.activation(ghi[:, :, :], gw, ACT.Copy).then_inc(ghi_ready, 1)
                    chunk(2)
                    chunk(3)
                    for k in range(8):
                        act.wait_ge(bias_mm, k + 1)
                        nc.scalar.activation(bias[:, 2 * k:2 * k + 2, :], ps[:, OB + k % 2, :].rearrange("p (a n) -> p a n", a=2),
                                             ACT.Copy).then_inc(bias_ready, 1)
                with act.Fori(4 if s == 0 else 2, NCH - 1) as c:
                    chunk(c)
                hidden_hi(f, NCH - 2)
                hi_static(u0 + 31)
                silu(f, u0, NCH - 1)
                hi_static(u0 + 32)
                hidden_hi(f, NCH - 1, xhi)
                hi_static(u0 + 33)

            def attend(kind, out_unit):
                n0, p0, N = STAGE0[kind], PAIR0[kind], STAGES[kind]
                per = 2 if kind == "nsa" else 1

                def exps(n):
                    b = n % PB
                    act.wait_ge(logits_ready, n + 1)
                    for a in range(2):
                        for t, (c0, c1) in enumerate(((0, P), (P, SCORES))):
                            p_ = prob[b][:, a, c0:c1]
                            last = nc.scalar.activation(p_, p_, ACT.Exp, bias=nmax[:, b, a, t:t + 1], scale=-1.0,
                                                        accum_out=ssum[:, b, a, t:t + 1])
                    last.then_inc(exp_done, 1)

                def heads_hi(k):
                    act.wait_ge(heads_mm, n0 + per * (k + 1))
                    nc.scalar.activation(xhi[:, k, :], ps[:, OB + k % 2, 0:S], ACT.Copy).then_inc(ohi_ready, 1)
                for i in range(N + LAG + 2):
                    if i >= LAG + 2 and (i - LAG - 1) % per == 0:
                        heads_hi((i - LAG - 1) // per - 1)
                    if i < N:
                        exps(n0 + i)
                    if i in (N, N + 2):
                        hi_static(out_unit + (i - N) // 2)

            act.dma_start(ident, consts[:, C_ID:C_ID + P]).then_inc(ident_in, 16)

            square(0, 0, 0)
            act.wait_ge(raw_in[0], 16)
            for cols, signal in ((slice(0, 1024), first_hi), (slice(1024, 2048), w_hi)):
                nc.scalar.activation(whi[:, 0, cols], raw[:, 0, cols], ACT.Copy).then_inc(signal, 1)
            split_x(0, 0)
            square(0, 0, 1)
            hi_static(1)
            split_x(0, 1)
            for s, kind in enumerate(KINDS):
                u0 = U0[s]
                if kind == "ffn":
                    ffn(s)
                else:
                    nproj = 10 if kind == "nsa" else 12

                    def evacuate(k):
                        act.wait_ge(unit_done, u0 + k + 1)
                        src = ps[:, GB + k % 2, :].rearrange("p (a n) -> p a n", a=2)
                        scale = 1.0
                        if kind == "nsa":
                            if k >= 6:
                                dst, scale = qT[:, 2 * (k - 6):2 * (k - 6) + 2, :], DH ** -0.5
                            else:
                                dst = [vN[:, 0], vN[:, 1], kcv[:, 0], kcv[:, 1], kN[:, 0], kN[:, 1]][k]
                        elif k < 4:
                            dst = vF[:, :, k * UC:(k + 1) * UC]
                        else:
                            halves, c = (qF, 2 * (k - 4)) if k < 8 else (kFs, 2 * (k - 8))
                            for r in range(2):
                                o_ = slice(64 * r, 64 * r + 64)
                                last = nc.scalar.activation(halves[r][o_, c:c + 2, :], src[o_], ACT.Copy, scale=DH ** -0.5 if k < 8 else 1.0)
                            last.then_inc(proj_ready, 1)
                            return
                        nc.scalar.activation(dst, src, ACT.Copy, scale=scale).then_inc(proj_ready, 1)
                    hi_static(u0 + 2)
                    for k in range(1, nproj):
                        evacuate(k - 1)
                        hi_static(u0 + k + 2)
                        if kind == "nsa" and k == 3:
                            act.wait_ge(gates_mm, 1)
                            nc.scalar.activation(gate_e, ps[0:48, OB, 0:S], ACT.Exp, scale=-1.0).then_inc(gate_exp, 1)
                        if kind == "nsa" and k in (6, 9):
                            kv = (k - 6) // 3
                            act.wait_ge(hid_mm, kv + 1)
                            if kv:
                                act.wait_ge(cmp_mm, 1)
                            for m in range(2):
                                last = nc.scalar.activation(hid[:, m, :], ps[:, MB, m * 64:m * 64 + G * NC], ACT.Gelu_apprx_tanh,
                                                            bias=smallT[:, 32 + 2 * kv + m:33 + 2 * kv + m])
                            last.then_inc(hid_ready, 1)
                        if kind == "fox" and k == 3:
                            act.wait_ge(f_step, 2)
                            nc.scalar.activation(fT[:, 2, :], fT[:, 1, :], ACT.Exp, scale=-1.0).then_inc(f_exp, 1)
                            act.wait_ge(f_exp, 1)
                            nc.scalar.activation(fT[:, 3, :], fT[:, 2, :], ACT.Ln, bias=1.0).then_inc(f_ln, 1)
                    evacuate(nproj - 1)
                    if kind == "nsa":
                        act.wait_ge(sc_logits, 1)
                        nc.scalar.activation(sc[:, :, :, :], sc[:, :, :, :], ACT.Exp).then_inc(sc_exp, 1)
                    attend(kind, u0 + nproj + 2)
                    hi_static(u0 + nproj + 4)
                square(s, 1, 0)
                if s + 1 < NSUB:
                    u = U0[s + 1] + 1
                    act.wait_ge(raw_in[u % RING], 16 * (u // RING + 1))
                    act.wait_ge(unit_done, u - RING + 1)
                    nc.scalar.activation(whi[:, u % RING, 0:1024], raw[:, u % RING, 0:1024], ACT.Copy).then_inc(second_hi, 1)
                    square(s + 1, 0, 0)
                    nc.scalar.activation(whi[:, u % RING, 1024:2048], raw[:, u % RING, 1024:2048], ACT.Copy).then_inc(w_hi, 1)
                square(s, 1, 1)
                if s + 1 < NSUB:
                    split_x(s + 1, 0)
                    square(s + 1, 0, 1)
                    split_x(s + 1, 1)

        @block.vector
        def _(dve):
            def lo(u, slot):
                dve.wait_ge(w_hi, u + 1)
                nc.vector.tensor_tensor(wlo[:, slot, :], raw[:, slot, :], whi[:, slot, :].bitcast(F32), ALU.subtract).then_inc(w_lo, 1)

            def lo_static(u):
                if u < NUNITS:
                    lo(u, u % RING)

            def gain_output(s, t):
                if t == 0:
                    dve.wait_ge(gpost_in, 16 * (s + 1))
                wait_output(dve, s, t)
                dve.wait_ge(sumsq, norm_index(s, 1, t) + 1)
                nc.vector.tensor_tensor(normed[:, t, :].rearrange("p (a n) -> p a n", a=2), ps[:, YB + 2 * t:YB + 2 * t + 2, :],
                                        g_post[:, :].rearrange("p (a n) -> p a n", a=2), ALU.mult).then_inc(yg_ready, 1)

            def add_output(s, t):
                i = norm_index(s, 1, t)
                dve.wait_ge(yg_ready, TT * s + t + 1)
                dve.wait_ge(rstd_ready, i + 1)
                for cols, signal in ((slice(0, 512), res_half), (slice(512, 1024), res_ready)):
                    nc.vector.scalar_tensor_tensor(res[:, t, cols], normed[:, t, cols], rstd[:, i:i + 1], res[:, t, cols],
                                                   ALU.mult, ALU.add).then_inc(signal, 1)

            def norm_input(s, t):
                i = norm_index(s, 0, t)
                if t == 0:
                    dve.wait_ge(gpre_in, 16 * (s + 1))
                dve.wait_ge(res_in[t] if s == 0 else res_ready, 16 if s == 0 else TT * (s - 1) + t + 1)
                dve.wait_ge(rstd_ready, i + 1)
                for cols in (slice(0, 512), slice(512, 1024)):
                    nc.vector.scalar_tensor_tensor(normed[:, t, cols], res[:, t, cols], rstd[:, i:i + 1], g_pre[:, cols],
                                                   ALU.mult, ALU.mult).then_inc(normed_ready, 1)

            def split_x(s, t):
                for b in range(2):
                    dve.wait_ge(xhi_ready, 4 * s + 2 * t + b + 1)
                    src = ps[:, GB + 2 * t + b, :].rearrange("p (k n) -> p k n", k=4)
                    at = (slice(None), slice(4 * b, 4 * b + 4), slice(t * P, (t + 1) * P))
                    nc.vector.tensor_tensor(xlo[at], src, xhi[at].bitcast(F32), ALU.subtract).then_inc(xlo_ready, 1)

            def hidden(f, u0, c, hi_=hhi, lo_=hlo, done=None):
                dve.wait_ge(unit_done, done or u0 + 2 + 3 * c)
                dve.wait_ge(silu_ready, NCH * f + c + 1)
                if not (isinstance(c, int) and c == 0 and f == 0):
                    dve.wait_ge(hlo_ready, NCH * f + c)
                nc.vector.tensor_tensor(prod_sb, silu_sb, ps[:, UB, :], ALU.mult).then_inc(prod_ready, 1)
                dve.wait_ge(hhi_ready, NCH * f + c + 1)
                src = ps[:, MB, :] if isinstance(c, int) and c == 0 else prod_sb
                nc.vector.tensor_tensor(lo_[:, 0:2, :], src.rearrange("p (a n) -> p a n", a=2), hi_[:, 0:2, :].bitcast(F32),
                                        ALU.subtract).then_inc(hlo_ready, 1)

            def ffn(s):
                f, u0 = FFN_OF[s], U0[s]

                def chunk(c):
                    hidden(f, u0, c - 1)
                    for k in (1, 2, 3):
                        if not isinstance(c, int) or u0 + 3 * c + k < NUNITS:
                            lo(u0 + k + 3 * c, (u0 + k) % RING)
                lo_static(u0 + 2)
                lo_static(u0 + 3)
                chunk(1)
                if s == 0:
                    dve.wait_ge(ghi_ready, 1)
                    nc.vector.tensor_tensor(glo[:, :, :], gw, ghi[:, :, :].bitcast(F32), ALU.subtract).then_inc(glo_ready, 1)
                    dve.wait_ge(pre_mm, 1)
                    nc.vector.tensor_copy(smallT[:, :], ps[:, MB, 0:36])
                    nc.vector.tensor_copy(vrev[:, :], ps[0:H, MB, 64:64 + SCORES]).then_inc(pre_evac, 1)
                    chunk(2)
                    chunk(3)
                with dve.Fori(4 if s == 0 else 2, NCH - 1) as c:
                    chunk(c)
                hidden(f, u0, NCH - 2)
                for k in (31, 32):
                    lo_static(u0 + k)
                hidden(f, u0, NCH - 1, xhi, xlo, u0 + 31)
                lo_static(u0 + 33)

            def attend(kind, out_unit, after_logits):
                n0, p0, N = STAGE0[kind], PAIR0[kind], STAGES[kind]
                per = 2 if kind == "nsa" else 1
                mask = cst[:, C_MASK:C_MASK + S]

                def logits(n):
                    b = n % PB
                    dve.wait_ge(scores_mm, n + 1)
                    if n >= PB:
                        dve.wait_ge(probT_mm, n - PB + 1)
                    for a in range(2):
                        for t, (c0, c1) in enumerate(((0, P), (P, SCORES))):
                            j0 = P if t == 0 else 0
                            add = bias[:, n, j0:S] if kind == "nsa" else mask[:, j0:S]
                            last = nc.vector.tensor_tensor_reduce(
                                out=prob[b][:, a, c0:c1], in0=ps[:, 2 * (n % 2) + a, c0:c1], in1=add, scale=-1.0, scalar=3e38,
                                op0=ALU.add, op1=ALU.min, accum_out=nmax[:, b, a, t:t + 1])
                    last.then_inc(logits_ready, 1)

                def factors(n):
                    b = n % PB
                    dve.wait_ge(exp_done, n + 1)
                    if kind == "nsa":
                        nc.vector.reciprocal(rsum[:, b], ssum[:, b]).then_inc(rsum_ready, 1)
                        dve.wait_ge(rsum_ready, n + 1)
                        g_ = gate[:, :, 16 + n:48:16].rearrange("p t a -> p a t")
                        nc.vector.tensor_tensor(fac[:, b], rsum[:, b], g_, ALU.mult).then_inc(fac_ready, 1)
                    else:
                        nc.vector.reciprocal(fac[:, b], ssum[:, b]).then_inc(fac_ready, 1)

                def probs_T(n):
                    b = n % 2
                    dve.wait_ge(probT_mm, n + 1)
                    if n >= 2:
                        dve.wait_ge(heads_mm, n - 1)
                    nc.vector.tensor_copy(probT[:, b], ps[:, GB:GB + 2, 0:SCORES]).then_inc(probT_ready, 1)

                def heads_lo(k):
                    dve.wait_ge(ohi_ready, p0 + k + 1)
                    nc.vector.tensor_tensor(xlo[:, k, :], ps[:, OB + k % 2, 0:S], xhi[:, k, :].bitcast(F32),
                                            ALU.subtract).then_inc(olo_ready, 1)
                for i in range(N + LAG + 2):
                    if i < N:
                        logits(n0 + i)
                    if i in after_logits:
                        after_logits[i]()
                    if i == N:
                        factors(n0 + i - 1)
                        lo_static(out_unit)
                    if i == N + 3:
                        lo_static(out_unit + 1)
                    if LAG <= i < N + LAG:
                        probs_T(n0 + i - LAG)
                    if 1 <= i < N:
                        factors(n0 + i - 1)
                    if i >= LAG + 2 and (i - LAG - 1) % per == 0:
                        heads_lo((i - LAG - 1) // per - 1)

            norm_input(0, 0)
            dve.wait_ge(first_hi, 1)
            nc.vector.tensor_tensor(wlo[:, 0, 0:1024], raw[:, 0, 0:1024], whi[:, 0, 0:1024].bitcast(F32), ALU.subtract)
            dve.wait_ge(w_hi, 1)
            nc.vector.tensor_tensor(wlo[:, 0, 1024:2048], raw[:, 0, 1024:2048], whi[:, 0, 1024:2048].bitcast(F32), ALU.subtract).then_inc(w_lo, 1)
            split_x(0, 0)
            norm_input(0, 1)
            lo_static(1)
            split_x(0, 1)
            for s, kind in enumerate(KINDS):
                u0 = U0[s]
                if kind == "ffn":
                    ffn(s)
                else:
                    nproj = 10 if kind == "nsa" else 12

                    def gather(kv):
                        dve.wait_ge(pairs_in[kv], 64)
                        if kv:
                            dve.wait_ge(hid_mm, 1)
                        src = pairsv[:, :, :]
                        src = bass.AP(pairs[:, :].tensor, pairs[:, :].offset, [list(pairs[:, :].ap[0]), [2, 16], [S, G], [CS, NC]])
                        pe_ = smallT[:, 16 * kv:16 * kv + 16]
                        pe_ = bass.AP(pe_.tensor, pe_.offset, [list(pe_.ap[0]), [1, 16], [0, G], [0, NC]])
                        dst = flat[:, 0:960].rearrange("p (k g c) -> p k g c", k=16, g=G)
                        nc.vector.tensor_tensor(dst, src, pe_, ALU.add).then_inc(flat_ready, 1)
                    lo_static(u0 + 2)
                    for k in range(1, nproj):
                        lo_static(u0 + k + 2)
                        if kind == "nsa":
                            if k == 4:
                                dve.wait_ge(gate_exp, 1)
                                nc.vector.tensor_scalar(gate_e, gate_e, 1.0, None, ALU.add).then_inc(gate_step, 1)
                                dve.wait_ge(gate_step, 1)
                                nc.vector.reciprocal(gateT, gate_e).then_inc(gate_ready, 1)
                            if k == 5:
                                gather(0)
                            if k == 6:
                                dve.wait_ge(gateT_mm, 1)
                                nc.vector.tensor_copy(gate[:, :, :], ps[:, OB, S:S + 96].rearrange("p (t n) -> p t n", t=TT)).then_inc(gate_ready, 1)
                            if k == 7:
                                dve.wait_ge(cmp_mm, 1)
                                dve.wait_ge(kcmp_zero, 1)
                                for r in range(2):
                                    half_ = slice(64 * r, 64 * r + 64)
                                    last = nc.vector.tensor_copy(kcmp[half_, :, r, :], ps[half_, MB, 128:128 + G * NC].rearrange("p (g c) -> p g c", g=G))
                                last.then_inc(cmp_ready, 1)
                            if k == 7:
                                gather(1)
                            if k == 9:
                                dve.wait_ge(hid_ready, 2)
                                dve.wait_ge(hidR_zero, 1)
                                for m in range(2):
                                    src = hid[:, m, :]
                                    src = bass.AP(src.tensor, src.offset, [list(src.ap[0]), [NC, G], [0, 4], [1, NC]])
                                    last = nc.vector.tensor_copy(hidR[:, m, :, :, 0:NC], src)
                                last.then_inc(hidR_ready, 1)
                        elif k == 3:
                            dve.wait_ge(gates_mm, 2)
                            dve.wait_ge(bf_in, 32)
                            nc.vector.tensor_scalar(fT[:, 0, :], ps[0:32, MB, 0:S], bf[:, :], None, ALU.add).then_inc(f_step, 1)
                            dve.wait_ge(f_step, 1)
                            nc.vector.scalar_tensor_tensor(fT[:, 1, :], fT[:, 0, :], -1.0, fT[:, 0, :], ALU.mult, ALU.max).then_inc(f_step, 1)
                        elif k == 4:
                            dve.wait_ge(f_ln, 1)
                            nc.vector.scalar_tensor_tensor(fT[:, 1, :], fT[:, 0, :], 0.0, fT[:, 3, :], ALU.min, ALU.subtract).then_inc(f_step, 1)
                            dve.wait_ge(f_step, 3)
                            nc.vector.memset(zeros, 0.0).then_inc(f_step, 1)
                            dve.wait_ge(f_step, 4)
                            nc.vector.tensor_tensor_scan(cum[:, :], zeros, fT[:, 1, :], 0.0, ALU.add, ALU.add).then_inc(cum_ready, 1)
                        elif k == 6:
                            dve.wait_ge(cum_mm, 1)
                            nc.vector.tensor_copy(cum_wide, ps[:, MB, 0:S]).then_inc(wide_ready, 1)
                        elif k == 7:
                            dve.wait_ge(wide_ready, 1)
                            for r in range(2):
                                o_ = slice(64 * (1 - r), 64 * (1 - r) + 64)
                                v = cum_wide[o_, :]
                                v = bass.AP(v.tensor, v.offset, [list(v.ap[0]), [0, KT], [1, S]])
                                nc.vector.tensor_scalar(kFs[r][o_, :, :], v, cst[o_, C_R:C_R + 1], cst[o_, C_R + 1:C_R + 2],
                                                        ALU.mult, ALU.add).then_inc(f_step, 1)
                    if kind == "nsa":
                        dve.wait_ge(cmp_mm, 2)
                        nc.vector.tensor_copy(vcmp[:, :, :], ps[:, MB, 192:448].rearrange("p (g d) -> p g d", g=G)).then_inc(cmp_ready, 1)
                        dve.wait_ge(sc_mm, 1)
                        s3 = sc[:, :, :, :].rearrange("p t h c -> p (t h) c")
                        c1 = (P - CB) // CS + 1
                        s_ = ps[:, OB, 0:TT * H * NC].rearrange("p (t h c) -> p t h c", t=TT, c=NC)
                        nc.vector.tensor_tensor(sc[:, 0, :, 0:c1], s_[:, 0, :, 0:c1], bias[:, :, P + CB - 1:S:CS], ALU.add)
                        nc.vector.tensor_scalar(sc[:, 0, :, c1:NC], s_[:, 0, :, c1:NC], NEG, None, ALU.add)
                        nc.vector.tensor_tensor(sc[:, 1, :, :], s_[:, 1], bias[:, :, CB - 1:S:CS], ALU.add).then_inc(sc_step, 1)
                        dve.wait_ge(sc_step, 1)
                        nc.vector.tensor_reduce(cmx[:, :, :].rearrange("p t h -> p (t h)"), s3, AX.X, ALU.max).then_inc(sc_step, 1)
                        dve.wait_ge(sc_step, 2)
                        def spread(v):
                            return bass.AP(v[:, :, :].tensor, v[:, :, :].offset, [list(v[:, :, :].ap[0]), [1, TT * H], [0, NC]])
                        nc.vector.tensor_tensor(s3, s3, spread(cmx), ALU.subtract).then_inc(sc_logits, 1)

                    def compressed_probs():
                        dve.wait_ge(sc_exp, 1)
                        nc.vector.tensor_reduce(csum[:, :, :].rearrange("p t h -> p (t h)"), s3, AX.X, ALU.add).then_inc(sc_step, 1)
                        dve.wait_ge(sc_step, 3)
                        nc.vector.reciprocal(cfac[:, :, :], csum[:, :, :]).then_inc(sc_step, 1)
                        dve.wait_ge(sc_step, 4)
                        for t in range(TT):
                            last = nc.vector.scalar_tensor_tensor(cfac[:, t, :], cfac[:, t, :], cst[:, C_VALID + t:C_VALID + t + 1],
                                                                  gate[:, t, 0:H], ALU.mult, ALU.mult)
                        last.then_inc(sc_step, 1)
                        dve.wait_ge(sc_step, 5)
                        dve.wait_ge(probc_zero, 1)
                        nc.vector.tensor_tensor(probc.rearrange("p t h c -> p (t h) c")[:, :, 0:NC], s3, spread(cfac), ALU.mult).then_inc(probc_ready, 1)

                    def compressed_transposed():
                        for t in range(TT):
                            dve.wait_ge(probcT_mm, t + 1)
                            nc.vector.tensor_copy(probcT[:, :, t * P:(t + 1) * P],
                                                  ps[:, MB - t, :].rearrange("p (g n) -> p g n", g=G)).then_inc(probcT_ready, 1)
                    attend(kind, u0 + nproj + 2, {0: compressed_probs, 2: compressed_transposed} if kind == "nsa" else {})
                    lo_static(u0 + nproj + 4)
                more = s + 1 < NSUB
                gain_output(s, 0)
                add_output(s, 0)
                if more:
                    u = U0[s + 1] + 1
                    dve.wait_ge(second_hi, s + 1)
                    nc.vector.tensor_tensor(wlo[:, u % RING, 0:1024], raw[:, u % RING, 0:1024], whi[:, u % RING, 0:1024].bitcast(F32), ALU.subtract)
                    norm_input(s + 1, 0)
                    gain_output(s, 1)
                    split_x(s + 1, 0)
                    add_output(s, 1)
                    dve.wait_ge(w_hi, u + 1)
                    nc.vector.tensor_tensor(wlo[:, u % RING, 1024:2048], raw[:, u % RING, 1024:2048], whi[:, u % RING, 1024:2048].bitcast(F32),
                                            ALU.subtract).then_inc(w_lo, 1)
                if more:
                    norm_input(s + 1, 1)
                    split_x(s + 1, 1)
                else:
                    gain_output(s, 1)
                    add_output(s, 1)

        @block.tensor
        def _(pe):
            def mm(out_, l, r, start, stop):
                return nc.tensor.matmul(out_, l, r, start=start, stop=stop)

            def split_mm(out_, l, r, start, stop):
                (lh, ll), (rh, rl) = l, r
                mm(out_, lh, rh, start, False)
                mm(out_, lh, rl, False, False)
                return mm(out_, ll, rh, False, stop)

            def wcols(slot):
                return [w[:, slot, :].rearrange("p (k n) -> p k n", k=KT) for w in (whi, wlo)]

            def wrows(slot):
                return [w[:, slot, :].rearrange("p (k n) -> p k n", k=2) for w in (whi, wlo)]

            def features(u, slot, bank, between=None):
                pe.wait_ge(w_lo, u + 1)
                wh, wl = wcols(slot)
                for a in range(2):
                    if a == 1 and between:
                        between()
                    for k in range(KT):
                        last = split_mm(ps[:, bank, a * S:(a + 1) * S], (wh[:, k, a * P:(a + 1) * P], wl[:, k, a * P:(a + 1) * P]),
                                        (xhi[:, k, :], xlo[:, k, :]), k == 0, k == KT - 1)
                last.then_inc(unit_done, 1)

            def tokens(u, slot, bank, tiles=(0, 1), x_parts=None, before={}):
                pe.wait_ge(w_lo, u + 1)
                wh, wl = wcols(slot)
                for t in tiles:
                    for k in range(KT):
                        if k in before:
                            before[k]()
                        if x_parts is not None and k in (0, 4):
                            pe.wait_ge(xlo_ready, x_parts + 1 + k // 4)
                        last = split_mm(ps[:, bank, t * UC:(t + 1) * UC], (xhi[:, k, t * P:(t + 1) * P], xlo[:, k, t * P:(t + 1) * P]),
                                        (wh[:, k, :], wl[:, k, :]), k == 0, k == KT - 1)
                if TT - 1 in tiles:
                    last.then_inc(unit_done, 1)

            def row_products(slot, left, k, t, first=False, final=False):
                wh, wl = wrows(slot)
                l = [v[:, t * P:(t + 1) * P] for v in left(k)]
                for b in range(2):
                    last = split_mm(ps[:, YB + 2 * t + b, :], l, (wh[:, k, 512 * b:512 * b + 512], wl[:, k, 512 * b:512 * b + 512]), first, final)
                return last

            def rows(u, slot, left, first):
                pe.wait_ge(w_lo, u + 1)
                for k in range(2):
                    for t in range(TT):
                        last = row_products(slot, left, k, t, first and k == 0)
                last.then_inc(unit_done, 1)

            def close_sublayer(u, lefts, inputs_ready):
                for t in range(TT):
                    for i in range(2):
                        if t == 0:
                            pe.wait_ge(w_lo, u + i + 1)
                            inputs_ready(i)
                        for k in range(2):
                            last = row_products((u + i) % RING, lefts[i], k, t, False, i == 1 and k == 1)
                        if t == 0:
                            if i == 1:
                                last.then_inc(y_ready, 1)
                        else:
                            last.then_inc(unit_done, 1)

            def transpose_input(s, t, halves=(0, 1)):
                for b in halves:
                    pe.wait_ge(normed_ready, 2 * (TT * s + t) + b + 1)
                    for k in range(4):
                        last = nc.tensor.transpose(ps[:, GB + 2 * t + b, k * P:(k + 1) * P], normed[:, t, (4 * b + k) * P:(4 * b + k + 1) * P], ident)
                    last.then_inc(xT_ready, 1)

            def hold_clock(n):
                for _ in range(n):
                    mm(ps[:, GB, 0:P], ident, ident, True, True)

            def open_sublayer(s):
                u0 = U0[s]
                hold_clock(IDLE_START if s == 0 else IDLE_BOUNDARY)
                transpose_input(s, 0)
                tokens(u0, u0 % RING, GB, (0,), 4 * s)
                tokens(u0 + 1, (u0 + 1) % RING, UB, (0,),
                       before={4: lambda: transpose_input(s, 1, (0,)), 6: lambda: transpose_input(s, 1, (1,))})
                tokens(u0, u0 % RING, GB, (1,), 4 * s + 2)
                tokens(u0 + 1, (u0 + 1) % RING, UB, (1,))

            def setup():
                pe.wait_ge(small_in, 32)
                pe.wait_ge(cst_in, 16)
                nc.tensor.transpose(ps[:, MB, 0:36], small[:, :], cst[0:36, C_ID:C_ID + 36])
                pe.wait_ge(tab_in, 32)
                pe.wait_ge(oh_in, 16)
                mm(ps[0:H, MB, 64:64 + SCORES], tab[:, :], back, True, True).then_inc(pre_mm, 1)

            def ffn(s):
                f, u0 = FFN_OF[s], U0[s]

                def first_T():
                    pe.wait_ge(prod_ready, NCH * f + 1)
                    for a in range(2):
                        for t in range(TT):
                            last = nc.tensor.transpose(ps[:, MB, a * S + t * P:a * S + (t + 1) * P],
                                                       prod_sb[:, t * UC + a * P:t * UC + (a + 1) * P], ident)
                    last.then_inc(prodT_mm, 1)

                def gate_(c, slot, first=False):
                    if not (isinstance(c, int) and c == 0):
                        pe.wait_ge(silu_ready, NCH * f + c)
                    features(gate_unit(u0, c), slot, GB, first_T if first else None)

                def up_(c, slot):
                    if not (isinstance(c, int) and c == 0):
                        pe.wait_ge(prod_ready, NCH * f + c)
                    features(u0 + 1 + 3 * c, slot, UB)

                def down_(c, slot, first=False):
                    pe.wait_ge(hlo_ready, NCH * f + c + 1)
                    rows(u0 + 3 + 3 * c, slot, lambda k: (hhi[:, k, :], hlo[:, k, :]), first)

                def chunk(c, first=False):
                    gate_(c, (u0 + 2) % RING, first)
                    down_(c - 1, u0 % RING, first)
                    up_(c, (u0 + 1) % RING)
                chunk(1, True)
                if s == 0:
                    setup()
                    chunk(2)
                    chunk(3)
                    pe.wait_ge(skew_in, 16)
                    for k in range(8):
                        if k >= 2:
                            pe.wait_ge(bias_ready, k - 1)
                        mm(ps[:, OB + k % 2, :], cst[:, C_J:C_J + P], skew[:, 2 * k:2 * k + 2, :], True, True).then_inc(bias_mm, 1)
                with pe.Fori(4 if s == 0 else 2, NCH - 1) as c:
                    chunk(c)
                gate_(NCH - 1, (u0 + 29) % RING)
                pe.wait_ge(prod_ready, NCH * f + NCH - 1)
                features(u0 + 30, (u0 + 30) % RING, UB)
                close_sublayer(u0 + 31, (lambda k: (hhi[:, k, :], hlo[:, k, :]), lambda k: (xhi[:, k, :], xlo[:, k, :])),
                               lambda i: pe.wait_ge(hlo_ready, NCH * f + NCH - 1 + i))

            def gates(bank, c0, c1):
                pe.wait_ge(glo_ready, 1)
                for k in range(KT):
                    last = split_mm(ps[0:c1 - c0, bank, 0:S], (ghi[:, k, c0:c1], glo[:, k, c0:c1]), (xhi[:, k, :], xlo[:, k, :]),
                                    k == 0, k == KT - 1)
                last.then_inc(gates_mm, 1)

            def compress_hidden(kv):
                pe.wait_ge(flat_ready, kv + 1)
                pe.wait_ge(w1_in[kv], 16)
                if kv:
                    pe.wait_ge(hid_ready, 1)
                    pe.wait_ge(cmp_ready, 1)
                for m in range(2):
                    for k in range(16):
                        last = mm(ps[:, MB, m * 64:m * 64 + G * NC], w1[:, k, m * P:(m + 1) * P], flatv[:, k, :], k == 0, k == 15)
                last.then_inc(hid_mm, 1)

            def compress_out(kv):
                if kv == 0:
                    pe.wait_ge(w2_in, 48)
                    pe.wait_ge(hid_ready, 1)
                    for m in range(2):
                        last = mm(ps[:, MB, 128:128 + G * NC], w2k[:, m, :, :].rearrange("p r d -> p (r d)"), hid[:, m, :], m == 0, m == 1)
                else:
                    pe.wait_ge(hidR_ready, 1)
                    for g in range(G):
                        for m in range(2):
                            last = mm(ps[:, MB, 192 + g * DH:192 + (g + 1) * DH], hidR[:, m, g, :, :].rearrange("p r c -> p (r c)"),
                                      w2v[:, m, :], m == 0, m == 1)
                last.then_inc(cmp_mm, 1)

            def attend(kind, after_scores, out_rows, projected):
                n0, p0, N = STAGE0[kind], PAIR0[kind], STAGES[kind]
                per = 2 if kind == "nsa" else 1

                def side(h):
                    return slice(64 * (h % 2), 64 * (h % 2) + 64)

                def keys(n, a):
                    if kind == "nsa":
                        h, g = n, n // G
                        k_ = kN if h % 2 == g % 2 else kX
                        return h, k_[side(h), a, g // 2, :]
                    h = 2 * (n - n0) + a
                    return h, kFs[a][:, h // 2, :]

                def values(n, a, t):
                    if kind == "nsa":
                        return vN[:, a, t, (n // G) * DH:(n // G + 1) * DH]
                    h = 2 * (n - n0) + a
                    return vF[:, t, h * DH:(h + 1) * DH]

                def scores(n):
                    b = n % 2
                    if n >= 2:
                        pe.wait_ge(logits_ready, n - 1)
                    for a in range(2):
                        h, k_ = keys(n, a)
                        for t, (c0, c1) in enumerate(((0, P), (P, SCORES))):
                            o_ = ps[:, 2 * b + a, c0:c1]
                            q_ = qT[side(h), h // 2, :] if kind == "nsa" else qF[a][:, h // 2, :]
                            last = mm(o_, q_[:, t * P:(t + 1) * P], k_[:, 0:c1 - c0], True, True)
                    last.then_inc(scores_mm, 1)

                def probs_T(n):
                    b = n % PB
                    pe.wait_ge(prob_ready, n + 1)
                    if n >= 1:
                        pe.wait_ge(probT_ready, n)
                    for a in range(2):
                        for k in range(3):
                            last = nc.tensor.transpose(ps[:, GB + a, k * P:(k + 1) * P], prob[b][:, a, k * P:(k + 1) * P], ident)
                    last.then_inc(probT_mm, 1)

                def heads(n):
                    b = n % 2
                    pe.wait_ge(probT_ready, n + 1)
                    pair = (n - n0) // per
                    if pair >= 2:
                        pe.wait_ge(olo_ready, p0 + pair - 1)
                    bank = OB + pair % 2
                    for a in range(2):
                        half_ = side(n) if kind == "nsa" else side(a)
                        start = kind == "fox" or a == 0
                        if kind == "nsa" and a == 0:
                            if n == n0:
                                pe.wait_ge(probcT_ready, 2)
                            r = 32 * (n % G)
                            mm(ps[half_, bank, 0:S], vcmp[r:r + 32, n // G, :], probcT[r:r + 32, n // G, :], True, False)
                            start = False
                        mm(ps[half_, bank, 0:S], values(n, a, 0), probT[:, b, a, 0:S], start, False)
                        last = mm(ps[half_, bank, P:S], values(n, a, 1), probT[:, b, a, S:SCORES], False, kind == "fox" or a == 1)
                    last.then_inc(heads_mm, 1)
                for i in range(N + LAG + 1):
                    if i < N:
                        scores(n0 + i)
                    if i in after_scores:
                        after_scores[i]()
                    if i == LAG:
                        pe.wait_ge(proj_ready, projected)
                    if i == N + 1:
                        pe.wait_ge(logits_ready, n0 + N)
                        out_rows(0)
                    if LAG <= i < N + LAG:
                        probs_T(n0 + i - LAG)
                    if i == N + LAG:
                        out_rows(1)
                    if i >= LAG + 1:
                        heads(n0 + i - LAG - 1)

            pe.wait_ge(ident_in, 16)
            for s, kind in enumerate(KINDS):
                u0 = U0[s]
                open_sublayer(s)
                if kind == "ffn":
                    ffn(s)
                    continue
                pr0 = PROJ0[kind]
                nproj = 10 if kind == "nsa" else 12
                for k in range(nproj):
                    if k >= 2:
                        pe.wait_ge(proj_ready, pr0 + k - 1)
                        by_token = kind == "fox" and k < 4
                        (tokens if by_token else features)(u0 + k, (u0 + k) % RING, GB + k % 2)
                    if kind == "nsa" and k == 2:
                        gates(OB, 0, 48)
                    if kind == "nsa" and k == 5:
                        pe.wait_ge(gate_ready, 1)
                        for t in range(TT):
                            last = nc.tensor.transpose(ps[:, OB, S + 48 * t:S + 48 * (t + 1)], gateT[:, t * P:(t + 1) * P], cst[0:48, C_ID:C_ID + 48])
                        last.then_inc(gateT_mm, 1)
                    if kind == "nsa" and k in (5, 8):
                        compress_hidden((k - 5) // 3)
                    if kind == "nsa" and k in (6, 9):
                        compress_out((k - 6) // 3)
                    if kind == "fox" and k == 1:
                        gates(MB, 48, GWC)
                    if kind == "fox" and k == 5:
                        pe.wait_ge(cum_ready, 1)
                        mm(ps[:, MB, 0:S], cst[0:2 * H, C_SEL:C_SEL + P], cum[:, :], True, True).then_inc(cum_mm, 1)
                pe.wait_ge(proj_ready, pr0 + nproj - 1)
                if kind == "nsa":
                    pe.wait_ge(kx_in, 64)

                    def compressed_scores():
                        pe.wait_ge(proj_ready, pr0 + nproj)
                        pe.wait_ge(gate_ready, 2)
                        pe.wait_ge(cmp_ready, 1)
                        for t in range(TT):
                            for pair in range(H // 2):
                                c0 = (t * H + 2 * pair) * NC
                                last = mm(ps[:, OB, c0:c0 + 2 * NC], qT[:, pair, t * P:(t + 1) * P], kcmp[:, 2 * pair // G, :, :], True, True)
                        last.then_inc(sc_mm, 1)

                    def compressed_T():
                        pe.wait_ge(probc_ready, 1)
                        pe.wait_ge(cmp_ready, 2)
                        for t in range(TT):
                            for g in range(G):
                                last = nc.tensor.transpose(ps[:, MB - t, g * P:(g + 1) * P],
                                                           probc[:, t, G * g:G * g + G, :].rearrange("p h c -> p (h c)"), ident)
                            last.then_inc(probcT_mm, 1)
                else:
                    pe.wait_ge(decay_ready, 1)
                    pe.wait_ge(f_step, 6)

                def heads_of(k):
                    return lambda j: (xhi[:, 2 * k + j, :], xlo[:, 2 * k + j, :])

                def out_rows(k):
                    pe.wait_ge(olo_ready, PAIR0[kind] + 2 * k + 2)
                    rows(u0 + nproj + k, (u0 + nproj + k) % RING, heads_of(k), k == 0)
                attend(kind, {0: compressed_scores, 2: compressed_T} if kind == "nsa" else {}, out_rows, pr0 + nproj)
                close_sublayer(u0 + nproj + 2, (heads_of(2), heads_of(3)),
                               lambda i: pe.wait_ge(olo_ready, PAIR0[kind] + 2 * (2 + i) + 2))


_INS = ["x", "norm_g", "ffn_w_gate", "ffn_w_up", "ffn_w_down", "rel_bias", "nsa_w_in", "nsa_cmp_pe",
        "nsa_cmp_w1", "nsa_cmp_b1", "nsa_cmp_w2", "nsa_w_out", "fox_w_in", "fox_b_f", "fox_w_out"]


def kernel(**inputs):
    import concourse.bacc as _bacc
    from concourse.bass_utils import run_bass_kernel_spmd as _run

    nc = _bacc.Bacc("TRN2", target_bir_lowering=False, num_devices=1)
    arrays, args = {}, []
    consts, onehots = tables()
    for name, a in [(n, inputs[n]) for n in _INS] + [("consts", consts), ("onehots", onehots)]:
        a = np.ascontiguousarray(a)
        arrays[f"in_{name}"] = a
        args.append(nc.dram_tensor(f"in_{name}", a.shape, mybir.dt.from_np(a.dtype), kind="ExternalInput").ap())
    args.append(nc.dram_tensor("out_0", (1, S, D), F32, kind="ExternalOutput").ap())
    args.append(nc.dram_tensor("scratch", (H, SCORES), F32, kind="Internal").ap())
    trunk(nc, *args)
    r = _run(nc, [arrays], core_ids=[0])
    return r.results[0]["out_0"]
```
